# Optimizing a Trainium2 kernel written in Bass

```python
import jax, jax.numpy as jnp
from jax import lax
import numpy as np

D_MODEL = 1024
BATCH = 1
SEQ = 1024
DEPTH = 2

CHUNK = 64
HEAD_DIM = 64
A_HEADS = 8
A_LEFT_CHUNKS = 8
A_MAX_REL = 256
B_Q_HEADS = 8
B_KV_HEADS = 2
B_GROUP = B_Q_HEADS // B_KV_HEADS
B_WINDOW = 128
B_LEFT_CHUNKS = B_WINDOW // CHUNK - 1
ROPE_THETA = 10000.0
RMS_EPS = 1e-6
WIDTH_A = A_HEADS * HEAD_DIM
WIDTH_B = B_Q_HEADS * HEAD_DIM
KV_WIDTH_B = B_KV_HEADS * HEAD_DIM
SPLITS = (WIDTH_A, WIDTH_A, WIDTH_A, WIDTH_A, WIDTH_B, KV_WIDTH_B, KV_WIDTH_B, WIDTH_B, D_MODEL, D_MODEL)
D_IN = sum(SPLITS)

kernel_name = "hybrid_chunked_relbias_swa_sink_gated_merge"

def rmsnorm(x, g):
    xf = x.astype(jnp.float32)
    y = xf * lax.rsqrt(jnp.mean(xf * xf, axis=-1, keepdims=True) + RMS_EPS)
    return (y * g.astype(jnp.float32)).astype(x.dtype)

def rope(t, pos):
    half = t.shape[-1] // 2
    inv_freq = ROPE_THETA ** (-jnp.arange(half, dtype=jnp.float32) / half)
    ang = pos.astype(jnp.float32)[..., None] * inv_freq
    cos = jnp.cos(ang)[:, :, None, :]
    sin = jnp.sin(ang)[:, :, None, :]
    tf = t.astype(jnp.float32)
    t1, t2 = tf[..., :half], tf[..., half:]
    return jnp.concatenate([t1 * cos - t2 * sin, t2 * cos + t1 * sin], axis=-1).astype(t.dtype)

def chunk_band(t, left):
    b, s = t.shape[0], t.shape[1]
    n = s // CHUNK
    tc = t.reshape((b, n, CHUNK) + t.shape[2:])
    tp = jnp.pad(tc, [(0, 0), (left, 0)] + [(0, 0)] * (tc.ndim - 2))
    idx = jnp.arange(n)[:, None] + jnp.arange(left + 1)[None, :]
    band = tp[:, idx]
    return band.reshape((b, n, (left + 1) * CHUNK) + t.shape[2:])

def band_valid(n, left):
    ok = (jnp.arange(n)[:, None] - left + jnp.arange(left + 1)[None, :]) >= 0
    return jnp.repeat(ok, CHUNK, axis=1)

def chunked_relbias_attention(q, k, v, table):
    b, s, h, d = q.shape
    n = s // CHUNK
    band = (A_LEFT_CHUNKS + 1) * CHUNK
    qc = q.reshape(b, n, CHUNK, h, d)
    kb = chunk_band(k, A_LEFT_CHUNKS)
    vb = chunk_band(v, A_LEFT_CHUNKS)
    scores = jnp.einsum('bnqhd,bnkhd->bhnqk', qc, kb, preferred_element_type=jnp.float32) * (d ** -0.5)
    rel = A_LEFT_CHUNKS * CHUNK + jnp.arange(CHUNK)[:, None] - jnp.arange(band)[None, :]
    rel_idx = jnp.clip(rel, -A_MAX_REL, A_MAX_REL) + A_MAX_REL
    bias = table.astype(jnp.float32)[:, rel_idx]
    scores = scores + bias[None, :, None, :, :]
    valid = band_valid(n, A_LEFT_CHUNKS)
    scores = jnp.where(valid[None, None, :, None, :], scores, -jnp.inf)
    p = jax.nn.softmax(scores, axis=-1).astype(v.dtype)
    out = jnp.einsum('bhnqk,bnkhd->bnqhd', p, vb)
    return out.reshape(b, s, h * d)

def sliding_window_sink_gqa(q, k, v, sink):
    b, s, h, d = q.shape
    n = s // CHUNK
    band = (B_LEFT_CHUNKS + 1) * CHUNK
    qc = q.reshape(b, n, CHUNK, B_KV_HEADS, B_GROUP, d)
    kb = chunk_band(k, B_LEFT_CHUNKS)
    vb = chunk_band(v, B_LEFT_CHUNKS)
    scores = jnp.einsum('bnqhgd,bnshd->bhgnqs', qc, kb, preferred_element_type=jnp.float32) * (d ** -0.5)
    valid = band_valid(n, B_LEFT_CHUNKS)
    scores = jnp.where(valid[None, None, None, :, None, :], scores, -jnp.inf)
    sk = sink.astype(jnp.float32).reshape(B_KV_HEADS, B_GROUP)
    sk = jnp.broadcast_to(sk[None, :, :, None, None, None], scores.shape[:-1] + (1,))
    p = jax.nn.softmax(jnp.concatenate([scores, sk], axis=-1), axis=-1)[..., :band].astype(v.dtype)
    out = jnp.einsum('bhgnqs,bnshd->bnqhgd', p, vb)
    return out.reshape(b, s, h * d)

def setup_inputs(seed: int = 0) -> dict:
    key = jax.random.key(seed)
    ks = jax.random.split(key, 10)
    x = jax.random.normal(ks[0], (BATCH, SEQ, D_MODEL), jnp.float32)
    offsets = jax.random.randint(ks[1], (BATCH,), 0, 100000, dtype=jnp.int32)
    positions = offsets[:, None] + jnp.arange(SEQ, dtype=jnp.int32)[None, :]
    norm_g = 1.0 + 0.05 * jax.random.normal(ks[2], (DEPTH, D_MODEL), jnp.float32)
    w_in = jax.random.normal(ks[3], (DEPTH, D_MODEL, D_IN), jnp.float32) * D_MODEL ** -0.5
    rel_bias = 0.5 * jax.random.normal(ks[4], (DEPTH, A_HEADS, 2 * A_MAX_REL + 1), jnp.float32)
    sinks = 0.5 * jax.random.normal(ks[5], (DEPTH, B_Q_HEADS), jnp.float32)
    w_a_out = jax.random.normal(ks[6], (DEPTH, WIDTH_A, D_MODEL), jnp.float32) * WIDTH_A ** -0.5
    w_b_out = jax.random.normal(ks[7], (DEPTH, WIDTH_B, D_MODEL), jnp.float32) * WIDTH_B ** -0.5
    w_out = jax.random.normal(ks[8], (DEPTH, D_MODEL, D_MODEL), jnp.float32) * D_MODEL ** -0.5
    final_g = 1.0 + 0.05 * jax.random.normal(ks[9], (D_MODEL,), jnp.float32)
    return {"x": x, "positions": positions, "norm_g": norm_g, "w_in": w_in,
            "rel_bias": rel_bias, "sinks": sinks, "w_a_out": w_a_out,
            "w_b_out": w_b_out, "w_out": w_out, "final_g": final_g}

def reference(x, positions, norm_g, w_in, rel_bias, sinks, w_a_out, w_b_out, w_out, final_g):
    b, s, _ = x.shape
    split_idx = [int(i) for i in np.cumsum(SPLITS)[:-1]]
    for l in range(DEPTH):
        h = rmsnorm(x, norm_g[l])
        proj = jnp.einsum('bsd,de->bse', h, w_in[l])
        qa, ka, va, za, qb, kb, vb, zb, ga, gb = jnp.split(proj, split_idx, axis=-1)
        ya = chunked_relbias_attention(qa.reshape(b, s, A_HEADS, HEAD_DIM),
                                       ka.reshape(b, s, A_HEADS, HEAD_DIM),
                                       va.reshape(b, s, A_HEADS, HEAD_DIM), rel_bias[l])
        ya = jnp.einsum('bse,ed->bsd', ya * jax.nn.silu(za), w_a_out[l])
        qbr = rope(qb.reshape(b, s, B_Q_HEADS, HEAD_DIM), positions)
        kbr = rope(kb.reshape(b, s, B_KV_HEADS, HEAD_DIM), positions)
        yb = sliding_window_sink_gqa(qbr, kbr, vb.reshape(b, s, B_KV_HEADS, HEAD_DIM), sinks[l])
        yb = jnp.einsum('bse,ed->bsd', yb * jax.nn.silu(zb), w_b_out[l])
        merged = jax.nn.sigmoid(ga) * ya + jax.nn.sigmoid(gb) * yb
        x = x + jnp.einsum('bsd,de->bse', merged, w_out[l])
    return rmsnorm(x, final_g)


_drawn_inputs = setup_inputs


def setup_inputs(seed=0):
    import zlib

    import numpy as np

    out = dict(_drawn_inputs(seed))
    spreads = {}
    factors = {'norm_g': 6.359, 'sinks': 8.0}
    for name, (base, spread) in spreads.items():
        noise = np.random.default_rng([zlib.crc32(name.encode()), seed]).standard_normal(out[name].shape)
        drawn = base * np.exp(spread * noise) if base else spread * noise
        out[name] = __import__('jax').numpy.asarray(drawn.astype(out[name].dtype))
    for name, factor in factors.items():
        out[name] = (out[name] * factor).astype(out[name].dtype)
    return out
```

```python
from contextlib import ExitStack

import concourse.bass as bass
import numpy as np
from concourse import mybir
from concourse.bass import ds

F32 = mybir.dt.float32
F32R = mybir.dt.float32r
I32 = mybir.dt.int32
ACT = mybir.ActivationFunctionType
ALU = mybir.AluOpType

P = 128
DEPTH = 2
SEQ = 1024
D = 1024
CHUNK = 64
HD = 64
HEADS = 8
A_LEFT = 4
B_LEFT = 1
A_MAX_REL = 256
WIDTH = HEADS * HD
KV_HEADS = 2
KVW = KV_HEADS * HD
D_IN = 4 * WIDTH + WIDTH + 2 * KVW + WIDTH + 2 * D
HALF = HD // 2
ROPE_THETA = 10000.0
EPS = 1e-6
SCALE = HD ** -0.5
BIG = 1e30

KC = D // P
ST = SEQ // P
HP = HEADS // 2
COL = dict(zip(("qA", "kA", "vA", "zA", "qB", "kB", "vB", "zB", "gA", "gB"),
               np.cumsum([0, WIDTH, WIDTH, WIDTH, WIDTH, WIDTH, KVW, KVW, WIDTH, D]).tolist()))

N_B = 6
N_V = 4
N_T = 8
N_Z = 8
N_M = 3 * KC
N_O = KC
W_B, W_V = 0, N_B
W_T = W_V + N_V
W_Z = W_T + N_T
W_M = W_Z + N_Z
W_O = W_M + N_M
NW = W_O + N_O
SLOTS = 4
RAW = 2

UB, UV, UT = 6, 4, 8
NU = UB + UV + UT
TILES = 2 * ST
SPLIT0, X_NEW0, O_DONE0, ZY0, SILU0, SIG0, MM0 = 2, 1, 1, 1, 2, 2, 3

TAB_STEPS = 18

PI2 = (6.25, 135 / 2 ** 12, 237 / 2 ** 20)
PI2 += (2 * np.pi - sum(PI2),)


def pipeline(eng, stages, steps, iters):
    for s in range(steps):
        for lag, stage in stages:
            if s >= lag:
                stage(0, s - lag)
    with eng.Fori(1, iters) as it:
        for s in range(steps):
            for lag, stage in stages:
                if s >= lag:
                    stage(it, s - lag)
                else:
                    stage(it - 1, s - lag + steps)
    for s in range(steps, steps + max(lag for lag, _ in stages)):
        for lag, stage in stages:
            if s - lag < steps:
                stage(iters - 1, s - lag)


def build(nc, x, positions, norm_g, w_in, rel_bias, sinks, w_a_out, w_b_out, w_out, final_g,
          rope_freq, out):
    ctx = ExitStack()
    with ctx:
        base = (nc.sbuf_base + 1023) // 1024 * 1024 - 512

        def at(name, shape, dt, kb):
            return nc.alloc_sbuf_tensor_at(name, shape, dt, offset=base + int(kb * 1024))

        def sem(name):
            return ctx.enter_context(nc.semaphore(name))

        def scratch(name, shape, dt):
            return nc.dram_tensor(name, shape, dt, kind="Internal").ap()

        hT_hi = at("hT_hi", [P, KC, SEQ], F32R, 0)
        hT_lo = at("hT_lo", [P, KC, SEQ], F32R, 32)
        mg_hi = at("mg_hi", [P, KC, SEQ], F32R, 0)
        mg_lo = at("mg_lo", [P, KC, SEQ], F32R, 32)
        xt = at("xt", [P, ST, D], F32, 64)
        xs = at("xs", [P, ST, D], F32, 96)
        yg_hi = at("yg_hi", [P, KC, SEQ], F32R, 64)
        yg_lo = at("yg_lo", [P, KC, SEQ], F32R, 96)
        q_st = [at(f"q_st{u}", [P, SEQ], F32R, 64 + 16 * u) for u in range(2)]
        k_st = [at(f"k_st{u}", [P, SEQ], F32R, 68 + 16 * u) for u in range(2)]
        k_sw = [at(f"k_sw{u}", [P, SEQ], F32R, 72 + 16 * u) for u in range(2)]
        v_hi = [at(f"v_hi{u}", [P, ST, HD], F32R, 76 + 16 * u) for u in range(2)]
        v_lo = [at(f"v_lo{u}", [P, ST, HD], F32R, 78 + 16 * u) for u in range(2)]
        pt_hi = {"A": at("ptA_hi", [P, 2, A_LEFT + 2, 256], F32R, 96),
                 "B": at("ptB_hi", [P, 2, B_LEFT + 2, 256], F32R, 96)}
        pt_lo = {"A": at("ptA_lo", [P, 2, A_LEFT + 2, 256], F32R, 108),
                 "B": at("ptB_lo", [P, 2, B_LEFT + 2, 256], F32R, 108)}
        SW = (A_LEFT + 1) * P
        s_at = [120, 122.625, 125.25, 184]
        s_buf = {"A": [at(f"sA{i}", [P, SW + 8], F32, s_at[i]) for i in range(4)],
                 "B": [at(f"sB{i}", [P, 2 * P + 8], F32, 120 + 1.25 * i) for i in range(4)]}
        bias = {"A": [at(f"biasA{u}", [P, SW], F32, 187 + 2.5 * u) for u in range(2)],
                "B": [at("maskB", [P, 2 * P], F32, 125.5)] * 2}
        w_hi = at("w_hi", [P, SLOTS, KC, P], F32R, 128)
        w_lo = at("w_lo", [P, SLOTS, KC, P], F32R, 144)
        w_raw = at("w_raw", [P, RAW, KC, P], F32, 160)
        stage_hi = at("stage_hi", [P, 2, SEQ], F32R, 168)
        stage_lo = at("stage_lo", [P, 2, SEQ], F32R, 176)
        r_cos = at("r_cos", [P, 4, 256], F32, 184)
        r_sin = at("r_sin", [P, 4, 256], F32, 188)
        rot = at("rot", [P, 2, 4, 256], F32, 192)
        y_raw = at("y_raw", [P, 2 * HP, SEQ], F32, 168)
        merged = at("merged", [P, KC, SEQ], F32, 168)
        sg = at("sg", [P, SEQ], F32, 200)
        cos_t = at("cos_t", [P, ST, HALF], F32, 204)
        sin_t = at("sin_t", [P, ST, HALF], F32, 205)
        ident = at("ident", [P, P], F32, 206)
        small = at("small", [P, 128], F32, 206.5)
        g_t = small[:, 0:16]
        g_now = small[:, 72:80]
        nsink = small[:, 16:32]
        ssq = small[:, 32:40]
        rms = small[:, 40:48]
        rstd = small[:, 48:56]
        nmax = small[:, 56:60]
        esum = small[:, 60:64]
        rinv = small[:, 64:68]
        pos_i = at("pos_i", [P, ST], I32, 168)
        pos_f = at("pos_f", [P, ST], F32, 168.25)
        freq = at("freq", [P, HALF], F32, 168.5)
        ang = at("ang", [P, 2, ST * HALF], F32, 169)
        turns = at("turns", [P, 2, ST * HALF], F32, 171)
        turns_i = at("turns_i", [P, 2, ST * HALF], I32, 173)
        wrap = at("wrap", [P, 2, ST * HALF], F32, 175)
        TW = 2 * A_MAX_REL + 1
        table = at("table", [DEPTH * HEADS, TW], F32, 177)
        EXT = SW + P - 1
        ext = at("ext", [DEPTH * HEADS, EXT], F32, 180)
        g_row = at("g_row", [P, D], F32, 168)

        acc = ctx.enter_context(nc.psum_tensor("acc", [P, 8, 512], F32))

        def pair(i):
            return acc[:, 2 * i:2 * i + 2, :]

        def flat(i):
            return pair(i).rearrange("p b c -> p (b c)")

        x_dram = scratch("x_dram", [SEQ, D], F32)
        qkA = [scratch(f"qkA_{s}", [HP, 2, P, SEQ], F32) for s in ("hi", "lo")]
        vA = [scratch(f"vA_{s}", [SEQ, WIDTH], F32) for s in ("hi", "lo")]
        qB = [scratch(f"qB_{s}", [WIDTH, SEQ], F32) for s in ("hi", "lo")]
        kB = [scratch(f"kB_{s}", [KVW, SEQ], F32) for s in ("hi", "lo")]
        vB = [scratch(f"vB_{s}", [SEQ, KVW], F32) for s in ("hi", "lo")]
        ext_dram = scratch("ext_dram", [DEPTH * HEADS, EXT + 1], F32)
        bias_dram = scratch("bias_dram", [DEPTH * HEADS, P, SW], F32)

        table_in = sem("table_in")
        const_in = sem("const_in")
        ext_ready = sem("ext_ready")
        ext_out = sem("ext_out")
        bias_out = sem("bias_out")
        ident_s = sem("ident_s")
        tab = sem("tab")
        tab_act = sem("tab_act")
        x_in = sem("x_in")
        x_saved = sem("x_saved")
        x_back = sem("x_back")
        raw_in = [sem(f"raw_in{i}") for i in range(RAW)]
        split_hi = sem("split_hi")
        split = sem("split")
        sq_done = sem("sq_done")
        ms_done = sem("ms_done")
        rt_done = sem("rt_done")
        rs_done = sem("rs_done")
        xs_done = sem("xs_done")
        ht_ps = sem("ht_ps")
        ht_hi = sem("ht_hi")
        ht_lo = sem("ht_lo")
        u_done = sem("u_done")
        rope_m = sem("rope_m")
        rope_o = sem("rope_o")
        rt_ps = sem("rt_ps")
        st_hi = sem("st_hi")
        st_lo = sem("st_lo")
        stored = [sem(f"stored{i}") for i in range(2)]
        filled = sem("filled")
        at_set = sem("at_set")
        unit_in = [sem(f"unit_in{i}") for i in range(2)]
        qk_done = sem("qk_done")
        sk_done = sem("sk_done")
        mx_done = sem("mx_done")
        ex_done = sem("ex_done")
        ri_done = sem("ri_done")
        pr_done = sem("pr_done")
        tr_done = sem("tr_done")
        ph_done = sem("ph_done")
        pl_done = sem("pl_done")
        av_done = sem("av_done")
        y_done = sem("y_done")
        z_done = sem("z_done")
        silu_done = sem("silu_done")
        zy_done = sem("zy_done")
        yg_h = sem("yg_h")
        yg_l = sem("yg_l")
        g_done = sem("g_done")
        yo_done = sem("yo_done")
        sig_done = sem("sig_done")
        mm_done = sem("mm_done")
        mg_h = sem("mg_h")
        mg_l = sem("mg_l")
        o_done = sem("o_done")
        x_new = sem("x_new")
        gain_in = sem("gain_in")
        fin_sq = sem("fin_sq")
        fin_ms = sem("fin_ms")
        fin_y = sem("fin_y")
        out_s = sem("out_s")

        PAIRS = TILES // 2
        ORDER = {"A": 0, "B": 1}
        LEFT = {"A": A_LEFT, "B": B_LEFT}
        WIDE = {"A": SW, "B": 2 * P}

        def tile_no(l, which, it, t):
            return (l * 2 + ORDER[which]) * HP * TILES + it * TILES + t

        def pair_no(l, which, it, a):
            return (l * 2 + ORDER[which]) * HP * PAIRS + it * PAIRS + a

        def unit_total(l, which, it):
            n_a, n_b = 16 * 10, 16 * 8
            before = l * HP * (n_a + n_b)
            return before + ((it + 1) * n_a if which == "A" else HP * n_a + (it + 1) * n_b)

        def stored_after(l, s, more=0):
            per_layer = 32 * (NU // 2) + 32
            return l * per_layer + 32 * (s // 2 + 1) + (32 if s >= UB - 2 else 0) + 32 * more

        def blocks(which, m):
            lo = max(0, m - LEFT[which])
            return lo, m - lo + 1

        def scores(which, t):
            m = t % ST
            nb = blocks(which, m)[1]
            wide = WIDE[which]
            return s_buf[which][t % 4], slice(wide - nb * P, wide), nb

        def is_first(it):
            return isinstance(it, int) and it == 0

        def used(l, n):
            if n < W_T:
                return u_done, l * NU + 2 * (n // 2) + 2
            if n < W_Z:
                return u_done, l * NU + UB + UV + (n - W_T) + 1
            if n < W_M:
                return z_done, l * N_Z + (n - W_Z) + 1
            if n < W_O:
                i, d = divmod(n - W_M, 3)
                return (yo_done, l * 2 * KC + 2 * i + 2) if d == 2 else (g_done, l * 2 * KC + 2 * i + d + 1)
            return o_done, l * KC + 2 * ((n - W_O) // 2) + 2 + O_DONE0

        held = {e: sem(f"held_{e}") for e in ("sp", "pool", "pe", "dve")}

        def hold(name, eng, s, value):
            eng.wait_ge(s, value)
            eng.sem_inc(held[name], 1)

        block = ctx.enter_context(nc.Block())

        @block.sync
        def _(sp):
            w_in_v = w_in.rearrange("l (k p) c -> p (l k) c", p=P)
            w_o_v = w_out.rearrange("l (k p) c -> p (l k) c", p=P)
            w_a_v = w_a_out.rearrange("l (k p) c -> p (l k) c", p=P)
            w_b_v = w_b_out.rearrange("l (k p) c -> p (l k) c", p=P)
            x_v = x.rearrange("b (m p) c -> p (b m) c", p=P)
            xd_v = x_dram.rearrange("(m p) c -> p m c", p=P)
            NH = KC // 2

            for m in range(ST):
                sp.dma_start(xt[:, m, :], x_v[:, m, :]).then_inc(x_in, 16)

            def load(l, n, slot, parts):
                hold("sp", sp, split, l * NW + n - RAW + 1 + SPLIT0)
                for h, src in enumerate(parts):
                    sp.dma_start(w_raw[:, slot, h * NH:(h + 1) * NH], src).then_inc(raw_in[slot], 16)

            def full(view, l, c0):
                return [view[:, ds(l * KC + h * NH, NH), ds(c0, P)] for h in range(2)]

            def load_in(l, n, c0):
                load(l, n, n % RAW, full(w_in_v, l, c0))

            def heads(l, which, it, u):
                s = unit_in[u]
                r = u * HD
                if which == "A":
                    q = [t[ds(it, 1), 0, r:r + HD, :].rearrange("a p s -> (a p) s") for t in qkA]
                    k = [t[ds(it, 1), 1, r:r + HD, :].rearrange("a p s -> (a p) s") for t in qkA]
                    v = [t.rearrange("(m p) c -> p m c", p=P)[:, :, ds(it * P + r, HD)] for t in vA]
                else:
                    g = it // 2
                    q = [t[ds(it * P + r, HD), :] for t in qB]
                    k = [t[ds(g * HD, HD), :] for t in kB]
                    v = [t.rearrange("(m p) c -> p m c", p=P)[:, :, ds(g * HD, HD)] for t in vB]
                for half in range(2):
                    rows = slice(half * HD, half * HD + HD)
                    sp.dma_start(q_st[u][rows, :].bitcast(F32), q[half]).then_inc(s, 16)
                    sp.dma_start(k_st[u][rows, :].bitcast(F32), k[half]).then_inc(s, 16)
                    sp.dma_start(k_sw[u][rows, :].bitcast(F32), k[1 - half]).then_inc(s, 16)
                sp.dma_start(v_hi[u][:, :, :].bitcast(F32), v[0]).then_inc(s, 16)
                sp.dma_start(v_lo[u][:, :, :].bitcast(F32), v[1]).then_inc(s, 16)
                if which == "A":
                    row = l * HEADS + 2 * it + u
                    for rows, cols in ((slice(0, CHUNK), slice(0, SW - CHUNK)),
                                       (slice(CHUNK, P), slice(CHUNK, SW))):
                        src = bias_dram[ds(row, 1), rows, cols].rearrange("a p c -> (a p) c")
                        sp.dma_start(bias["A"][u][rows, cols], src).then_inc(s, 16)

            def next_heads(l, which, it):
                for u in range(2):
                    hold("sp", sp, av_done, pair_no(l, which, it - 1, 4 * (u + 1)))
                    heads(l, which, it, u)

            sp.wait_ge(ext_ready, 2)
            sp.dma_start(ext_dram[:, 0:EXT], ext[:, :]).then_inc(ext_out, 16)

            sp.wait_ge(ext_out, 16)
            for r in range(DEPTH):
                src = bass.AP(ext_dram.tensor, r * HEADS * (EXT + 1) + P - 1, [[EXT + 1, HEADS], [-1, P], [1, SW]])
                sp.dma_start(bias_dram[r * HEADS:(r + 1) * HEADS], src).then_inc(bias_out, 16)

            with sp.Fori(0, DEPTH) as l:
                for n in range(2):
                    load_in(l, n, COL["qB"] + P * n)
                sp.wait_ge(x_in, 16 * ST)
                sp.wait_ge(x_new, l * KC + X_NEW0)
                for m in range(ST):
                    sp.dma_start(xd_v[:, m, :], xt[:, m, :]).then_inc(x_saved, 16)
                for n in range(2, N_B):
                    load_in(l, n, COL["qB"] + P * n)
                for n in range(N_V):
                    load_in(l, W_V + n, COL["vA"] + P * n)
                for n in range(N_T):
                    load_in(l, W_T + n, (n % 2) * WIDTH + P * (n // 2))
                for n in range(2):
                    load_in(l, W_Z + n, COL["zA"] + P * n)
                sp.wait_ge(x_saved, 16 * ST * (l + 1))
                for s in (UB + UV, UB + UV + 1):
                    sp.wait_ge(stored[s % 2], stored_after(l, s))
                sp.wait_ge(bias_out, 16 * DEPTH)
                for u in range(2):
                    heads(l, "A", 0, u)
                for n in range(2, 4):
                    load_in(l, W_Z + n, COL["zA"] + P * n)
                for s in (NU - 2, NU - 1):
                    hold("sp", sp, stored[s % 2], stored_after(l, s))
                with sp.Fori(1, HP) as it:
                    next_heads(l, "A", it)
                for u in range(2):
                    hold("sp", sp, av_done, pair_no(l, "A", HP - 1, 4 * (u + 1)))
                    heads(l, "B", 0, u)
                for it in range(1, HP):
                    next_heads(l, "B", it)
                for n in range(4, N_Z):
                    load_in(l, W_Z + n, COL["zB"] + P * (n - 4))
                with sp.Fori(0, KC // 4) as ib:
                    for j in range(4):
                        n = W_M + 3 * (4 * ib + j)
                        c0 = (4 * ib + j) * P
                        slot = (W_M + 3 * j) % RAW
                        load(l, n, slot, full(w_in_v, l, COL["gA"] + c0))
                        load(l, n + 1, 1 - slot, full(w_in_v, l, COL["gB"] + c0))
                        load(l, n + 2, slot, [v[:, ds(l * NH, NH), ds(c0, P)] for v in (w_a_v, w_b_v)])
                for n in range(2):
                    load(l, W_O + n, (W_O + n) % RAW, full(w_o_v, l, P * n))
                sp.wait_ge(yo_done, 2 * KC * (l + 1))
                for m in range(ST):
                    sp.dma_start(xt[:, m, :], xd_v[:, m, :]).then_inc(x_back, 16)
                for n in range(2, N_O):
                    load(l, W_O + n, (W_O + n) % RAW, full(w_o_v, l, P * n))
            sp.wait_ge(mg_l, DEPTH * KC)
            sp.dma_start(g_row[:, :], final_g.rearrange("(a c) -> a c", a=1).to_broadcast([P, D])
                         ).then_inc(gain_in, 16)
            o_v = out.rearrange("b (m p) c -> p (b m) c", p=P)
            for m in range(ST):
                sp.wait_ge(fin_y, m + 1)
                sp.dma_start(o_v[:, m, :], xs[:, m, :]).then_inc(out_s, 16)
            sp.wait_ge(out_s, 16 * ST)

        @block.gpsimd
        def _(pool):
            for s, v in ((split, SPLIT0), (x_new, X_NEW0), (o_done, O_DONE0), (zy_done, ZY0),
                         (silu_done, SILU0), (sig_done, SIG0), (mm_done, MM0)):
                pool.sem_inc(s, v)
            pool.memset(ident[:, :], 0.0).then_inc(ident_s, 1)
            pool.wait_ge(ident_s, 1)
            pool.affine_select(out=ident[:, :], in_=ident[:, :], compare_op=ALU.not_equal, fill=1.0,
                               base=0, pattern=[[-1, P]], channel_multiplier=1).then_inc(ident_s, 1)

            def split_block(l, n):
                raw, hi, lo = w_raw[:, n % RAW], w_hi[:, n % SLOTS], w_lo[:, n % SLOTS]
                pool.wait_ge(raw_in[n % RAW], 32 * (l * (NW // 2) + n // 2 + 1))
                if n < 2:
                    pool.wait_ge(o_done, l * KC + O_DONE0)
                elif n >= SLOTS:
                    pool.wait_ge(*used(l, n - SLOTS))
                pool.sem_inc(held["pool"], 1)
                pool.tensor_scalar(hi, raw, 1.0, 1.0, ALU.mult, ALU.mult).then_inc(split_hi, 1)
                pool.wait_ge(split_hi, l * NW + n + 1)
                pool.tensor_tensor(lo, raw, hi.bitcast(F32), ALU.subtract).then_inc(split, 1)

            def probs(l, which, it, t):
                buf, cols, _ = scores(which, t)
                i = t % 4
                hold("pool", pool, ri_done, tile_no(l, which, it, t) + 1)
                pool.tensor_scalar(buf[:, cols], buf[:, cols], rinv[:, i:i + 1], 1.0,
                                   ALU.mult, ALU.mult).then_inc(pr_done, 1)

            def fill(l, n, rows, cols, buf, value):
                pool.memset(buf[rows, cols], value).then_inc(filled, 1)
                hold("pool", pool, filled, l * FILLS + n + 1)

            def zeros(l, n, which):
                for t in (pt_hi[which], pt_lo[which]):
                    for b in range(2):
                        pool.memset(t[:, b, LEFT[which] + 1, 0:P].bitcast(F32), 0.0)
                        last = pool.memset(t[:, b, 0, P:2 * P].bitcast(F32), 0.0)
                last.then_inc(filled, 1)
                hold("pool", pool, filled, l * FILLS + n + 1)

            early, late, every = slice(0, CHUNK), slice(CHUNK, P), slice(0, P)
            first, last = slice(0, CHUNK), slice(SW - CHUNK, SW)
            fills_a = [(rows, cols, b, -BIG) for b in bias["A"] for rows, cols in ((late, first), (early, last))]
            c4 = [slice(j * CHUNK, j * CHUNK + CHUNK) for j in range(4)]
            fills_b = [(every, c4[0], bias["B"][0], -BIG), (every, c4[2], bias["B"][0], 0.0),
                       (early, c4[1], bias["B"][0], 0.0), (late, c4[1], bias["B"][0], -BIG),
                       (early, c4[3], bias["B"][0], -BIG), (late, c4[3], bias["B"][0], 0.0)]
            FILLS = len(fills_a) + len(fills_b) + 2

            with pool.Fori(0, DEPTH) as l:
                for n in range(W_T + 2):
                    split_block(l, n)
                hold("pool", pool, st_lo, l * NU + UB)
                zeros(l, 0, "A")
                for n, f in enumerate(fills_a):
                    fill(l, 1 + n, *f)
                pool.sem_inc(at_set, 1)
                for n in range(W_T + 2, W_Z + 2):
                    split_block(l, n)
                pipeline(pool, [(0, lambda it, t: probs(l, "A", it, t))], TILES, HP)
                hold("pool", pool, av_done, pair_no(l, "B", 0, 0))
                zeros(l, 1 + len(fills_a), "B")
                for n, f in enumerate(fills_b):
                    fill(l, 2 + len(fills_a) + n, *f)
                pool.sem_inc(at_set, 1)
                pipeline(pool, [(0, lambda it, t: probs(l, "B", it, t))], TILES, HP)
                for n in range(W_Z + 2, NW):
                    split_block(l, n)

        @block.tensor
        def _(pe):
            def mm3(dst, stat, mov, first, last):
                pe.matmul(dst, stat[0], mov[0], start=first, stop=False)
                pe.matmul(dst, stat[0], mov[1], start=False, stop=False)
                return pe.matmul(dst, stat[1], mov[0], start=False, stop=last)

            def t_unit(c, chunks, mov, at_chunk, banks):
                for h in range(2):
                    cols = slice(h * 512, h * 512 + 512)
                    for i, k in enumerate(chunks):
                        mm = mm3(pair(banks)[:, h, :],
                                 [w[:, c % SLOTS, k, :] for w in (w_hi, w_lo)],
                                 [t[:, at_chunk + i, cols] for t in mov],
                                 i == 0, i == len(chunks) - 1)
                return mm

            def rows_unit(c, stat, half, banks):
                two = slice(c % SLOTS, c % SLOTS + 2)
                for j in range(4):
                    rows = slice((4 * half + j) * P, (4 * half + j) * P + P)
                    for k in range(KC):
                        mm = mm3(flat(banks)[:, 256 * j:256 * j + 256], [t[:, k, rows] for t in stat],
                                 [w[:, two, k, :] for w in (w_hi, w_lo)], k == 0, k == KC - 1)
                return mm

            hT = (hT_hi, hT_lo)

            def rotated(l, u):
                pe.wait_ge(rope_o, l * 2 * UB + 2 * u + 2)
                if u >= 2:
                    pe.wait_ge(st_lo, l * NU + u - 1)
                for cb in range(2 if u < UB - 2 else 1):
                    for j in range(4):
                        mm = pe.transpose(pair(2 + u % 2)[:, cb, j * P:j * P + P],
                                          rot[:, u % 2, j, cb * P:cb * P + P], ident[:, :])
                mm.then_inc(rt_ps, 1)

            def qk(l, which, it, t):
                u, m = divmod(t, ST)
                lo, nb = blocks(which, m)
                if m == 0:
                    pe.wait_ge(unit_in[u], unit_total(l, which, it))
                if not (which == "A" and is_first(it) and t < 2):
                    pe.wait_ge(mx_done, tile_no(l, which, it, t) - 1)
                w = max(nb, 2) * P
                for i, (a, b) in enumerate([(0, w)] if w <= 512 else [(0, w // 2), (w // 2, w)]):
                    dst = pair(t % 2)[:, i, 0:b - a]
                    keys = slice(lo * P + a, lo * P + b)
                    q = q_st[u][:, m * P:m * P + P]
                    pe.matmul(dst, q, k_st[u][:, keys], start=True, stop=False)
                    mm = pe.matmul(dst, q, k_sw[u][:, keys], start=False, stop=True)
                mm.then_inc(qk_done, 1)

            def tr(l, which, it, t):
                buf, cols, nb = scores(which, t)
                no = tile_no(l, which, it, t)
                pe.wait_ge(pr_done, no + 1)
                if not (which == "A" and is_first(it) and t == 0):
                    pe.wait_ge(pl_done, no)
                for i in range(nb):
                    a = cols.start + i * P
                    mm = pe.transpose(flat(2)[:, i * P:i * P + P], buf[:, a:a + P], ident[:, :])
                mm.then_inc(tr_done, 1)

            def av(l, which, it, t):
                if t % 2 == 0:
                    return
                u, m = divmod(t, ST)
                a = m // 2
                no = pair_no(l, which, it, t // 2)
                pe.wait_ge(pl_done, tile_no(l, which, it, t) + 1)
                if not (which == "A" and is_first(it) and t < 4):
                    pe.wait_ge(y_done, no - 1)
                dst = acc[0:HD, 6 + a % 2, 0:256]
                slots = range(max(0, LEFT[which] - 2 * a), LEFT[which] + 2)
                for i in slots:
                    j = 2 * a - LEFT[which] + i
                    mm = mm3(dst, (v_hi[u][:, j, :], v_lo[u][:, j, :]),
                             [t_[:, a % 2, i, :] for t_ in (pt_hi[which], pt_lo[which])],
                             i == slots[0], i == slots[-1])
                mm.then_inc(av_done, 1)

            pe.wait_ge(ident_s, 2)
            with pe.Fori(0, DEPTH) as l:
                for h in range(2):
                    pe.wait_ge(xs_done, l * ST + 4 * h + 4)
                    for k in range(KC):
                        if h == 1:
                            pe.wait_ge(ht_lo, l * 2 * KC + k + 1)
                        for j in range(4):
                            mm = pe.transpose(acc[:, k, j * P:j * P + P],
                                              xs[:, 4 * h + j, k * P:k * P + P], ident[:, :])
                        mm.then_inc(ht_ps, 1)
                pe.wait_ge(ht_lo, (l + 1) * 2 * KC)
                for u in range(UB + UV):
                    if u % 2 == 0:
                        pe.wait_ge(split, l * NW + u + 2 + SPLIT0)
                    if u >= 2 and u < UB:
                        pe.wait_ge(rope_m, l * 2 * UB + 2 * (u - 2) + 2)
                    if u >= UB:
                        pe.wait_ge(st_lo, l * NU + u - 1)
                    rows_unit(u - u % 2, hT, u % 2, u % 2).then_inc(u_done, 1)
                    if 1 <= u <= UB:
                        rotated(l, u - 1)
                with pe.Fori(0, N_T // 4) as ib:
                    for j in range(4):
                        pe.wait_ge(split, l * NW + W_T + 4 * ib + j + 1 + SPLIT0)
                        pe.wait_ge(st_lo, l * NU + UB + UV + 4 * ib + j - 1)
                        t_unit(W_T + j, range(KC), hT, 0, j % 2).then_inc(u_done, 1)
                pe.wait_ge(st_lo, (l + 1) * NU)
                pe.wait_ge(at_set, 2 * l + 1)
                for which in "AB":
                    if which == "B":
                        hold("pe", pe, at_set, 2 * l + 2)
                    pipeline(pe, [(0, lambda it, t: qk(l, which, it, t)),
                                  (2, lambda it, t: tr(l, which, it, t)),
                                  (4, lambda it, t: av(l, which, it, t))], TILES, HP)
                hold("pe", pe, mx_done, tile_no(l + 1, "A", 0, 0))
                with pe.Fori(0, N_Z // 4) as ib:
                    for j in range(4):
                        b = 4 * ib + j
                        pe.wait_ge(split, l * NW + W_Z + b + 1 + SPLIT0)
                        pe.wait_ge(silu_done, l * N_Z + b - 1 + SILU0)
                        t_unit(W_Z + j, range(KC), hT, 0, j % 2).then_inc(z_done, 1)
                pe.wait_ge(silu_done, (l + 1) * N_Z + SILU0)
                hold("pe", pe, y_done, pair_no(l + 1, "A", 0, 0))
                with pe.Fori(0, KC // 4) as ib:
                    for j in range(4):
                        i = 4 * ib + j
                        c = W_M + 3 * j
                        for br in range(2):
                            pe.wait_ge(split, l * NW + W_M + 3 * i + br + 1 + SPLIT0)
                            pe.wait_ge(sig_done, l * 2 * KC + 2 * i + br - 1 + SIG0)
                            t_unit(c + br, range(KC), hT, 0, 2 * br).then_inc(g_done, 1)
                            if br == 0:
                                pe.wait_ge(split, l * NW + W_M + 3 * i + 3 + SPLIT0)
                                pe.wait_ge(yg_l, (l + 1) * N_Z)
                            pe.wait_ge(mm_done, l * 3 * KC + 3 * (i - 1) + br + 1 + MM0)
                            t_unit(c + 2, range(4 * br, 4 * br + 4), (yg_hi, yg_lo), 4 * br,
                                   2 * br + 1).then_inc(yo_done, 1)
                pe.wait_ge(mg_l, (l + 1) * KC)
                for f in range(N_O):
                    if f % 2 == 0:
                        pe.wait_ge(split, l * NW + W_O + f + 2 + SPLIT0)
                    if f >= 4:
                        pe.wait_ge(x_new, l * KC + f - 3 + X_NEW0)
                    rows_unit(W_O + f - f % 2, (mg_hi, mg_lo), f % 2, f % 4).then_inc(o_done, 1)

        @block.scalar
        def _(act):
            copy = ACT.Copy
            for dst, src in ((pos_i[:, :], positions.rearrange("b (m p) -> p (b m)", p=P)),
                             (freq[:, :], rope_freq.rearrange("(a c) -> a c", a=1).to_broadcast([P, HALF])),
                             (g_t, norm_g.rearrange("l (k p) -> p (l k)", p=P)),
                             (nsink, sinks.rearrange("l h -> (l h)").rearrange("(a c) -> a c", a=1)
                              .to_broadcast([P, DEPTH * HEADS]))):
                with nc.allow_non_contiguous_dma(reason="a few KB"):
                    act.dma_start(dst, src).then_inc(const_in, 16)
            act.dma_start(table[:, :], rel_bias.rearrange("l h r -> (l h) r")).then_inc(table_in, 16)
            act.wait_ge(tab, TAB_STEPS)
            act.activation(sin_t[:, :, :].rearrange("p m c -> p (m c)"), ang[:, 0, :], ACT.Sin).then_inc(tab_act, 1)
            act.activation(cos_t[:, :, :].rearrange("p m c -> p (m c)"), ang[:, 1, :], ACT.Sin).then_inc(tab_act, 1)
            act.wait_ge(ext_out, 16)

            def exps(l, which, it, t):
                buf, cols, _ = scores(which, t)
                i = t % 4
                end = cols.stop + (1 if which == "B" else 0)
                act.wait_ge(mx_done, tile_no(l, which, it, t) + 1)
                act.activation(buf[:, cols.start:end], buf[:, cols.start:end], ACT.Exp,
                               bias=nmax[:, i:i + 1], scale=-1.0,
                               accum_out=esum[:, i:i + 1]).then_inc(ex_done, 1)

            def p_hi(l, which, it, t):
                m = t % ST
                a, tt = m // 2, m % 2
                lo, nb = blocks(which, m)
                s0 = lo - (2 * a - LEFT[which])
                act.wait_ge(tr_done, tile_no(l, which, it, t) + 1)
                if not (which == "A" and is_first(it) and t < 4):
                    act.wait_ge(av_done, pair_no(l, which, it, t // 2) - 1)
                act.activation(pt_hi[which][:, a % 2, s0:s0 + nb, tt * P:tt * P + P],
                               flat(2)[:, 0:nb * P].rearrange("p (n c) -> p n c", c=P),
                               copy).then_inc(ph_done, 1)

            def y_out(l, which, it, t):
                if t % 2 == 0:
                    return
                u, m = divmod(t, ST)
                a = m // 2
                act.wait_ge(av_done, pair_no(l, which, it, t // 2) + 1)
                act.activation(y_raw[u * HD:u * HD + HD, ds(ORDER[which] * HP + it, 1), a * 256:a * 256 + 256]
                               .rearrange("p a c -> p (a c)"),
                               acc[0:HD, 6 + a % 2, 0:256], copy).then_inc(y_done, 1)

            def stage(l, u, c, ib=0):
                act.wait_ge(st_lo, l * NU + u + 1)
                for i, (st, v_, qk_, q_, k_, vb_) in enumerate(
                        zip((stage_hi, stage_lo), vA, qkA, qB, kB, vB)):
                    s = stored[c % 2]
                    half = c % 2
                    src = st[:, c % 2, :].bitcast(F32)
                    if c < UB - 2:
                        rows, cols = slice(256 * (c // 2), 256 * (c // 2) + 256), slice(512 * half, 512 * half + 512)
                        act.dma_start(q_[rows, cols].rearrange("(b p) s -> p b s", p=P),
                                      src.rearrange("p (b s) -> p b s", b=2)).then_inc(s, 16)
                    elif c < UB:
                        act.dma_start(k_[:, 512 * half:512 * half + 512], src[:, 0:512]).then_inc(s, 16)
                        act.dma_start(vb_.rearrange("(m p) c -> p m c", p=P)[:, 4 * half:4 * half + 4, :],
                                      src[:, 512:1024].rearrange("p (m c) -> p m c", m=4)).then_inc(s, 16)
                    elif c < UB + UV:
                        c0 = 256 * ((c - UB) // 2)
                        act.dma_start(v_.rearrange("(m p) c -> p m c", p=P)[:, 4 * half:4 * half + 4, c0:c0 + 256],
                                      src.rearrange("p (m c) -> p m c", m=4)).then_inc(s, 16)
                    else:
                        t = c - UB - UV
                        act.dma_start(qk_[ds(2 * ib + t // 2, 1), t % 2].rearrange("a p s -> (a p) s"),
                                      src).then_inc(s, 16)

            with act.Fori(0, DEPTH) as l:
                act.wait_ge(x_in, 16 * ST)
                act.wait_ge(x_new, l * KC + X_NEW0)
                for m in range(ST):
                    act.activation(xs[:, m, :], xt[:, m, :], ACT.Square,
                                   accum_out=ssq[:, m:m + 1]).then_inc(sq_done, 1)
                act.wait_ge(ms_done, l + 1)
                act.activation(rms, rms, ACT.Sqrt).then_inc(rt_done, 1)
                for i in range(2 * KC):
                    h, k = divmod(i, KC)
                    act.wait_ge(ht_ps, l * 2 * KC + i + 1)
                    act.activation(hT_hi[:, k, h * 512:h * 512 + 512], acc[:, k, :], copy,
                                   scale=g_now[:, k:k + 1]).then_inc(ht_hi, 1)
                for u in range(UB + UV):
                    if u >= 2:
                        act.wait_ge(stored[u % 2], stored_after(l, u - 2))
                    if u < UB - 2:
                        act.wait_ge(rt_ps, l * UB + u + 1)
                        act.activation(stage_hi[:, u % 2, :], flat(2 + u % 2), copy).then_inc(st_hi, 1)
                    elif u < UB:
                        act.wait_ge(rt_ps, l * UB + u + 1)
                        act.activation(stage_hi[:, u % 2, 0:512], pair(2 + u % 2)[:, 0, :], copy)
                        act.activation(stage_hi[:, u % 2, 512:1024].rearrange("p (m c) -> p m c", m=4),
                                       flat(u % 2).rearrange("p (m c) -> p m c", m=4)[:, :, P:2 * P],
                                       copy).then_inc(st_hi, 1)
                    else:
                        act.wait_ge(u_done, l * NU + u + 1)
                        act.activation(stage_hi[:, u % 2, :], flat(u % 2), copy).then_inc(st_hi, 1)
                    stage(l, u, u)
                with act.Fori(0, N_T // 4) as ib:
                    for j in range(4):
                        c = UB + UV + j
                        act.wait_ge(stored[j % 2], stored_after(l, c - 2, 2 * ib))
                        act.wait_ge(u_done, l * NU + c + 4 * ib + 1)
                        act.activation(stage_hi[:, j % 2, :], flat(j % 2), copy).then_inc(st_hi, 1)
                        stage(l, c + 4 * ib, c, ib)
                for s in (NU - 2, NU - 1):
                    act.wait_ge(stored[s % 2], stored_after(l, s))
                for which in "AB":
                    act.wait_ge(at_set, 2 * l + 1 + ORDER[which])
                    pipeline(act, [(0, lambda it, t: exps(l, which, it, t)),
                                   (2, lambda it, t: p_hi(l, which, it, t)),
                                   (5, lambda it, t: y_out(l, which, it, t))], TILES, HP)
                def gated_hi(b):
                    act.wait_ge(zy_done, l * N_Z + b + 1 + ZY0)
                    act.activation(yg_hi[:, ds(b, 1), :].rearrange("p a c -> p (a c)"),
                                   y_raw[:, ds(b, 1), :].rearrange("p a c -> p (a c)"), copy).then_inc(yg_h, 1)

                with act.Fori(0, N_Z // 4) as ib:
                    for j in range(4):
                        b = 4 * ib + j
                        act.wait_ge(z_done, l * N_Z + b + 1)
                        act.wait_ge(zy_done, l * N_Z + b + ZY0)
                        act.activation(sg[:, :], flat(j % 2), ACT.Silu).then_inc(silu_done, 1)
                        gated_hi(b)
                with act.Fori(0, KC) as i:
                    for br in range(2):
                        act.wait_ge(g_done, l * 2 * KC + 2 * i + br + 1)
                        act.wait_ge(mm_done, l * 3 * KC + 3 * i + br + MM0)
                        act.activation(sg[:, :], flat(2 * br), ACT.Sigmoid).then_inc(sig_done, 1)
                act.wait_ge(g_done, (l + 1) * 2 * KC)
                with act.Fori(0, KC) as i:
                    act.wait_ge(mm_done, l * 3 * KC + 3 * i + 3 + MM0)
                    act.activation(mg_hi[:, ds(i, 1), :].rearrange("p a c -> p (a c)"),
                                   merged[:, ds(i, 1), :].rearrange("p a c -> p (a c)"), copy).then_inc(mg_h, 1)
            act.wait_ge(x_new, DEPTH * KC + X_NEW0)
            for m in range(ST):
                act.activation(xs[:, m, :], xt[:, m, :], ACT.Square,
                               accum_out=ssq[:, m:m + 1]).then_inc(fin_sq, 1)
            act.wait_ge(fin_ms, 1)
            act.activation(rms, rms, ACT.Sqrt).then_inc(fin_ms, 1)

        @block.vector
        def _(dve):
            dve.wait_ge(table_in, 16)
            far = SW - CHUNK * 2 + P - 1 - A_MAX_REL
            dve.tensor_scalar(ext[:, 0:far], table[:, TW - 1:TW].to_broadcast([DEPTH * HEADS, far]),
                              1 / SCALE, None, ALU.mult).then_inc(ext_ready, 1)
            dve.tensor_scalar(ext[:, far:EXT], table[:, TW - 1:TW - 1 - (EXT - far):-1], 1 / SCALE, None,
                              ALU.mult).then_inc(ext_ready, 1)
            dve.wait_ge(const_in, 64)
            n = [0]

            def step(ins):
                n[0] += 1
                ins.then_inc(tab, 1)
                dve.wait_ge(tab, n[0])

            a0, a1 = ang[:, 0, :], ang[:, 1, :]
            tn, tn_i, wr = turns[:, 0, :], turns_i[:, 0, :], wrap[:, 0, :]
            step(dve.tensor_scalar(nsink, nsink, -1.0, None, ALU.mult))
            step(dve.tensor_copy(pos_f[:, :], pos_i[:, :]))
            step(dve.tensor_tensor(a0.rearrange("p (m c) -> p m c", m=ST),
                                   pos_f[:, :].unsqueeze(2).to_broadcast([P, ST, HALF]),
                                   freq[:, :].unsqueeze(1).to_broadcast([P, ST, HALF]), ALU.mult))
            step(dve.tensor_scalar(tn, a0, 1 / (2 * np.pi), None, ALU.mult))
            step(dve.tensor_copy(tn_i, tn))
            step(dve.tensor_copy(tn, tn_i))
            for part in PI2:
                step(dve.scalar_tensor_tensor(out=a0, in0=tn, scalar=-part, in1=a0, op0=ALU.mult, op1=ALU.add))
            for a, op, lim in ((a0, ALU.is_gt, np.pi), (a0, ALU.is_lt, -np.pi), (a1, ALU.is_gt, np.pi)):
                if a is a1:
                    step(dve.tensor_scalar(a1, a0, np.pi / 2, None, ALU.add))
                step(dve.tensor_scalar(wr, a, lim, -2 * lim, op, ALU.mult))
                step(dve.tensor_tensor(a, a, wr, ALU.add))
            step(dve.tensor_scalar(ang[:, :, :], ang[:, :, :], 3.1415925, -3.1415925, ALU.min, ALU.max))
            assert n[0] == TAB_STEPS

            def maxes(l, which, it, t):
                buf, cols, nb = scores(which, t)
                no = tile_no(l, which, it, t)
                i = t % 4
                b = bias[which][t // ST]
                if not (which == "A" and is_first(it) and t < 4):
                    dve.wait_ge(tr_done, no - 3)
                if which == "B":
                    row = l * HEADS + 2 * it + t // ST
                    dve.sem_inc(held["dve"], 1)
                    dve.tensor_copy(buf[:, cols.stop:cols.stop + 1], nsink[:, ds(row, 1)]).then_inc(sk_done, 1)
                    dve.wait_ge(sk_done, (l * HP + it) * TILES + t + 1)
                    start = buf[:, cols.stop:cols.stop + 1]
                else:
                    start = 3e38
                hold("dve", dve, qk_done, no + 1)
                out_, in1, in0 = buf[:, cols], b[:, cols], flat(t % 2)[:, 0:nb * P]
                if nb * P > 512:
                    out_, in1 = [v.rearrange("p (h c) -> p h c", h=2) for v in (out_, in1)]
                    in0 = pair(t % 2)[:, :, 0:nb * P // 2]
                dve.tensor_tensor_reduce(out_, in0, in1, -SCALE, start, ALU.add, ALU.min,
                                         nmax[:, i:i + 1]).then_inc(mx_done, 1)

            def recips(l, which, it, t):
                i = t % 4
                dve.wait_ge(ex_done, tile_no(l, which, it, t) + 1)
                dve.reciprocal(rinv[:, i:i + 1], esum[:, i:i + 1]).then_inc(ri_done, 1)

            def p_lo(l, which, it, t):
                m = t % ST
                a, tt = m // 2, m % 2
                lo, nb = blocks(which, m)
                s0 = lo - (2 * a - LEFT[which])
                where = (slice(None), a % 2, slice(s0, s0 + nb), slice(tt * P, tt * P + P))
                dve.wait_ge(ph_done, tile_no(l, which, it, t) + 1)
                dve.tensor_tensor(pt_lo[which][where], flat(2)[:, 0:nb * P].rearrange("p (n c) -> p n c", c=P),
                                  pt_hi[which][where].bitcast(F32), ALU.subtract).then_inc(pl_done, 1)

            def rope(l, u):
                h = u % 2
                wide = 8 if u < UB - 2 else 4
                ps = flat(h).rearrange("p (m g c) -> p m g c", m=4, c=HALF)[:, :, 0:wide, :]
                dve.wait_ge(u_done, l * NU + u + 1)
                for dst, tb in ((r_cos, cos_t), (r_sin, sin_t)):
                    dve.tensor_tensor(dst[:, :, :].rearrange("p m (g c) -> p m g c", c=HALF)[:, :, 0:wide, :], ps,
                                      tb[:, 4 * h:4 * h + 4, :].unsqueeze(2).to_broadcast([P, 4, wide, HALF]),
                                      ALU.mult).then_inc(rope_m, 1)
                dve.wait_ge(rope_m, l * 2 * UB + 2 * u + 2)
                if u >= 2:
                    dve.wait_ge(rt_ps, l * UB + u - 1)
                c4, s4, r4 = [v.rearrange("p m (g t c) -> p m g t c", t=2, c=HALF)[:, :, 0:wide // 2]
                              for v in (r_cos[:, :, :], r_sin[:, :, :], rot[:, u % 2])]
                dve.tensor_tensor(r4[:, :, :, 0], c4[:, :, :, 0], s4[:, :, :, 1], ALU.subtract).then_inc(rope_o, 1)
                dve.tensor_tensor(r4[:, :, :, 1], c4[:, :, :, 1], s4[:, :, :, 0], ALU.add).then_inc(rope_o, 1)
                dve.wait_ge(rope_o, l * 2 * UB + 2 * u + 2)

            def lo_of(l, u, c):
                s = c % 2
                dve.wait_ge(st_hi, l * NU + u + 1)
                hi, lo = stage_hi[:, s, :].bitcast(F32), stage_lo[:, s, :]
                if c < UB - 2:
                    dve.tensor_tensor(lo, flat(2 + s), hi, ALU.subtract).then_inc(st_lo, 1)
                elif c < UB:
                    dve.tensor_tensor(lo[:, 0:512], pair(2 + s)[:, 0, :], hi[:, 0:512], ALU.subtract)
                    dve.tensor_tensor(lo[:, 512:1024].rearrange("p (m c) -> p m c", m=4),
                                      flat(s).rearrange("p (m c) -> p m c", m=4)[:, :, P:2 * P],
                                      hi[:, 512:1024].rearrange("p (m c) -> p m c", m=4),
                                      ALU.subtract).then_inc(st_lo, 1)
                else:
                    dve.tensor_tensor(lo, flat(s), hi, ALU.subtract).then_inc(st_lo, 1)

            dve.wait_ge(tab_act, 2)
            with dve.Fori(0, DEPTH) as l:
                dve.tensor_copy(g_now, g_t.rearrange("p (l k) -> p l k", l=DEPTH)[:, ds(l, 1), :]
                                .rearrange("p a k -> p (a k)"))
                dve.wait_ge(sq_done, (l + 1) * ST)
                dve.tensor_scalar(rms, ssq, 1 / D, EPS, ALU.mult, ALU.add).then_inc(ms_done, 1)
                dve.wait_ge(rt_done, l + 1)
                dve.reciprocal(rstd, rms).then_inc(rs_done, 1)
                dve.wait_ge(rs_done, l + 1)
                for m in range(ST):
                    dve.tensor_scalar(xs[:, m, :], xt[:, m, :], rstd[:, m:m + 1], None,
                                      ALU.mult).then_inc(xs_done, 1)
                for i in range(2 * KC):
                    h, k = divmod(i, KC)
                    cols = slice(h * 512, h * 512 + 512)
                    dve.wait_ge(ht_hi, l * 2 * KC + i + 1)
                    dve.scalar_tensor_tensor(out=hT_lo[:, k, cols], in0=acc[:, k, :], scalar=g_now[:, k:k + 1],
                                             in1=hT_hi[:, k, cols].bitcast(F32), op0=ALU.mult,
                                             op1=ALU.subtract).then_inc(ht_lo, 1)
                for u in range(UB):
                    rope(l, u)
                    if u >= 1:
                        lo_of(l, u - 1, u - 1)
                for u in range(UB - 1, UB + UV):
                    lo_of(l, u, u)
                with dve.Fori(0, N_T // 4) as ib:
                    for j in range(4):
                        lo_of(l, UB + UV + 4 * ib + j, UB + UV + j)
                for which in "AB":
                    dve.wait_ge(at_set, 2 * l + 1 + ORDER[which])
                    if which == "B":
                        dve.wait_ge(tr_done, tile_no(l, "B", 0, 0))
                    pipeline(dve, [(1, lambda it, t: recips(l, which, it, t)),
                                   (0, lambda it, t: maxes(l, which, it, t)),
                                   (3, lambda it, t: p_lo(l, which, it, t))], TILES, HP)
                with dve.Fori(0, N_Z) as b:
                    y = y_raw[:, ds(b, 1), :].rearrange("p a c -> p (a c)")
                    dve.wait_ge(silu_done, l * N_Z + b + 1 + SILU0)
                    dve.wait_ge(y_done, pair_no(l + 1, "A", 0, 0))
                    dve.tensor_tensor(y, y, sg[:, :], ALU.mult).then_inc(zy_done, 1)
                    dve.wait_ge(yg_h, l * N_Z + b + 1)
                    dve.tensor_tensor(yg_lo[:, ds(b, 1), :].rearrange("p a c -> p (a c)"), y,
                                      yg_hi[:, ds(b, 1), :].rearrange("p a c -> p (a c)").bitcast(F32),
                                      ALU.subtract).then_inc(yg_l, 1)
                with dve.Fori(0, KC) as i:
                    mg = merged[:, ds(i, 1), :].rearrange("p a c -> p (a c)")
                    base_mm = l * 3 * KC + 3 * i + MM0
                    for br, dst in enumerate((mg, sg[:, :])):
                        dve.wait_ge(sig_done, l * 2 * KC + 2 * i + br + 1 + SIG0)
                        dve.wait_ge(yo_done, l * 2 * KC + 2 * i + br + 1)
                        dve.tensor_tensor(dst, flat(2 * br + 1), sg[:, :], ALU.mult).then_inc(mm_done, 1)
                    dve.wait_ge(mm_done, base_mm + 2)
                    dve.tensor_tensor(mg, mg, sg[:, :], ALU.add).then_inc(mm_done, 1)
                with dve.Fori(0, KC) as i:
                    dve.wait_ge(mg_h, l * KC + i + 1)
                    dve.tensor_tensor(mg_lo[:, ds(i, 1), :].rearrange("p a c -> p (a c)"),
                                      merged[:, ds(i, 1), :].rearrange("p a c -> p (a c)"),
                                      mg_hi[:, ds(i, 1), :].rearrange("p a c -> p (a c)").bitcast(F32),
                                      ALU.subtract).then_inc(mg_l, 1)
                dve.wait_ge(x_back, 16 * ST * (l + 1))
                for f in range(N_O):
                    c0, h = 256 * (f // 2), f % 2
                    dve.wait_ge(o_done, l * KC + f + 1 + O_DONE0)
                    xv = xt[:, 4 * h:4 * h + 4, c0:c0 + 256]
                    dve.tensor_tensor(xv, flat(f % 4).rearrange("p (m c) -> p m c", m=4), xv,
                                      ALU.add).then_inc(x_new, 1)
            dve.wait_ge(fin_sq, ST)
            dve.tensor_scalar(rms, ssq, 1 / D, EPS, ALU.mult, ALU.add).then_inc(fin_ms, 1)
            dve.wait_ge(fin_ms, 2)
            dve.reciprocal(rstd, rms).then_inc(fin_ms, 1)
            dve.wait_ge(fin_ms, 3)
            dve.wait_ge(gain_in, 16)
            for m in range(ST):
                dve.scalar_tensor_tensor(out=xs[:, m, :], in0=xt[:, m, :], scalar=rstd[:, m:m + 1],
                                         in1=g_row[:, :], op0=ALU.mult, op1=ALU.mult).then_inc(fin_y, 1)


_INS = ["x", "positions", "norm_g", "w_in", "rel_bias", "sinks", "w_a_out", "w_b_out", "w_out", "final_g"]


def kernel(**inputs):
    import concourse.bacc as _bacc
    from concourse.bass_utils import run_bass_kernel_spmd as _run

    nc = _bacc.Bacc("TRN2", target_bir_lowering=False, num_devices=1)
    arrays, args = {}, []
    values = [(name, np.ascontiguousarray(inputs[name])) for name in _INS]
    values.append(("rope_freq", (ROPE_THETA ** (-np.arange(HALF) / HALF)).astype(np.float32)))
    for name, a in values:
        arrays[f"in_{name}"] = a
        args.append(nc.dram_tensor(f"in_{name}", a.shape, mybir.dt.from_np(a.dtype), kind="ExternalInput").ap())
    out = nc.dram_tensor("out_0", (1, SEQ, D), F32, kind="ExternalOutput").ap()
    build(nc, *args, out)
    r = _run(nc, [arrays], core_ids=[0])
    return r.results[0]["out_0"]
```

```python
from contextlib import ExitStack

import concourse.bass as bass
import numpy as np
from concourse import mybir
from concourse.bass import ds

F32 = mybir.dt.float32
F32R = mybir.dt.float32r
I32 = mybir.dt.int32
ACT = mybir.ActivationFunctionType
ALU = mybir.AluOpType

P = 128
DEPTH = 2
SEQ = 1024
D = 1024
CHUNK = 64
HD = 64
HEADS = 8
A_LEFT = 4
B_LEFT = 1
A_MAX_REL = 256
WIDTH = HEADS * HD
KV_HEADS = 2
KVW = KV_HEADS * HD
D_IN = 4 * WIDTH + WIDTH + 2 * KVW + WIDTH + 2 * D
HALF = HD // 2
ROPE_THETA = 10000.0
EPS = 1e-6
SCALE = HD ** -0.5
BIG = 1e30

KC = D // P
ST = SEQ // P
HP = HEADS // 2
COL = dict(zip(("qA", "kA", "vA", "zA", "qB", "kB", "vB", "zB", "gA", "gB"),
               np.cumsum([0, WIDTH, WIDTH, WIDTH, WIDTH, WIDTH, KVW, KVW, WIDTH, D]).tolist()))

N_B = 6
N_V = 4
N_T = 8
N_Z = 8
N_M = 3 * KC
N_O = KC
W_B, W_V = 0, N_B
W_T = W_V + N_V
W_Z = W_T + N_T
W_M = W_Z + N_Z
W_O = W_M + N_M
NW = W_O + N_O
SLOTS = 4
RAW = 2

UB, UV, UT = 6, 4, 8
NU = UB + UV + UT
TILES = 2 * ST
SPLIT0, X_NEW0, O_DONE0, ZY0, SILU0, SIG0, MM0 = 2, 1, 1, 1, 2, 2, 3

TAB_STEPS = 18

PI2 = (6.25, 135 / 2 ** 12, 237 / 2 ** 20)
PI2 += (2 * np.pi - sum(PI2),)


LAG = {"A": {"qk": 0, "mx": 0, "ex": 0, "ri": 1, "tr": 2, "hi": 2, "lo": 3, "av": 4, "y": 5},
       "B": {"qk": 0, "mx": 0, "ex": 0, "ri": 2, "tr": 4, "hi": 4, "lo": 5, "av": 6, "y": 7}}


def pipeline(eng, stages, steps, iters):
    for s in range(steps):
        for lag, stage in stages:
            if s >= lag:
                stage(0, s - lag)
    with eng.Fori(1, iters) as it:
        for s in range(steps):
            for lag, stage in stages:
                if s >= lag:
                    stage(it, s - lag)
                else:
                    stage(it - 1, s - lag + steps)
    for s in range(steps, steps + max(lag for lag, _ in stages)):
        for lag, stage in stages:
            if s - lag < steps:
                stage(iters - 1, s - lag)


def build(nc, x, positions, norm_g, w_in, rel_bias, sinks, w_a_out, w_b_out, w_out, final_g,
          rope_freq, out):
    ctx = ExitStack()
    with ctx:
        base = (nc.sbuf_base + 1023) // 1024 * 1024 - 512

        def at(name, shape, dt, kb):
            return nc.alloc_sbuf_tensor_at(name, shape, dt, offset=base + int(kb * 1024))

        def sem(name):
            return ctx.enter_context(nc.semaphore(name))

        def scratch(name, shape, dt):
            return nc.dram_tensor(name, shape, dt, kind="Internal").ap()

        hT_hi = at("hT_hi", [P, KC, SEQ], F32R, 0)
        hT_lo = at("hT_lo", [P, KC, SEQ], F32R, 32)
        mg_hi = at("mg_hi", [P, KC, SEQ], F32R, 0)
        mg_lo = at("mg_lo", [P, KC, SEQ], F32R, 32)
        xt = at("xt", [P, ST, D], F32, 64)
        xs = at("xs", [P, ST, D], F32, 96)
        yg_hi = at("yg_hi", [P, KC, SEQ], F32R, 64)
        yg_lo = at("yg_lo", [P, KC, SEQ], F32R, 96)
        q_st = [at(f"q_st{u}", [P, SEQ], F32R, 64 + 16 * u) for u in range(2)]
        k_st = [at(f"k_st{u}", [P, SEQ], F32R, 68 + 16 * u) for u in range(2)]
        k_sw = [at(f"k_sw{u}", [P, SEQ], F32R, 72 + 16 * u) for u in range(2)]
        v_st = [at(f"v_st{u}", [P, 2, ST, HD], F32R, 76 + 16 * u) for u in range(2)]
        PT = {"A": 2, "B": 4}
        pt_hi = {"A": at("ptA_hi", [P, PT["A"], A_LEFT + 2, 256], F32R, 96),
                 "B": at("ptB_hi", [P, PT["B"], B_LEFT + 2, 256], F32R, 96)}
        pt_lo = {"A": at("ptA_lo", [P, PT["A"], A_LEFT + 2, 256], F32R, 108),
                 "B": at("ptB_lo", [P, PT["B"], B_LEFT + 2, 256], F32R, 108)}
        SW = (A_LEFT + 1) * P
        s_at = [120, 122.625, 125.25, 184]
        s_buf = {"A": [at(f"sA{i}", [P, SW + 8], F32, s_at[i]) for i in range(4)],
                 "B": [at(f"sB{i}", [P, 2 * P + 8], F32, kb) for i, kb in
                       enumerate([120 + 33 / 32 * i for i in range(5)] + [200 + 33 / 32 * i for i in range(3)])]}
        bias = {"A": [at(f"biasA{u}", [P, SW], F32, 187 + 2.5 * u) for u in range(2)],
                "B": [at("maskB", [P, 2 * P], F32, 125.5)] * 2}
        w_hi = at("w_hi", [P, SLOTS, KC, P], F32R, 128)
        w_lo = at("w_lo", [P, SLOTS, KC, P], F32R, 144)
        w_raw = at("w_raw", [P, RAW, KC, P], F32, 160)
        stage_hi = at("stage_hi", [P, 2, SEQ], F32R, 168)
        stage_lo = at("stage_lo", [P, 2, SEQ], F32R, 176)
        r_cos = at("r_cos", [P, 4, 256], F32, 184)
        r_sin = at("r_sin", [P, 4, 256], F32, 188)
        rot = at("rot", [P, 2, 4, 256], F32, 192)
        y_raw = at("y_raw", [P, 2 * HP, SEQ], F32, 168)
        merged = at("merged", [P, KC, SEQ], F32, 168)
        sg = at("sg", [P, SEQ], F32, 200)
        cos_t = at("cos_t", [P, ST, HALF], F32, 204)
        sin_t = at("sin_t", [P, ST, HALF], F32, 205)
        ident = at("ident", [P, P], F32, 206)
        small = at("small", [P, 128], F32, 206.5)
        g_t = small[:, 0:16]
        g_now = small[:, 72:80]
        nsink = small[:, 16:32]
        ssq = small[:, 32:40]
        rms = small[:, 40:48]
        rstd = small[:, 48:56]
        nmax = small[:, 80:88]
        esum = small[:, 88:96]
        rinv = small[:, 96:104]
        rsq = small[:, 56:64]
        pos_i = at("pos_i", [P, ST], I32, 168)
        pos_f = at("pos_f", [P, ST], F32, 168.25)
        freq = at("freq", [P, HALF], F32, 168.5)
        ang = at("ang", [P, 2, ST * HALF], F32, 169)
        turns = at("turns", [P, 2, ST * HALF], F32, 171)
        turns_i = at("turns_i", [P, 2, ST * HALF], I32, 173)
        wrap = at("wrap", [P, 2, ST * HALF], F32, 175)
        TW = 2 * A_MAX_REL + 1
        table = at("table", [DEPTH * HEADS, TW], F32, 177)
        EXT = SW + P - 1
        ext = at("ext", [DEPTH * HEADS, EXT], F32, 180)
        g_row = at("g_row", [P, D], F32, 168)

        acc = ctx.enter_context(nc.psum_tensor("acc", [P, 8, 512], F32))

        def pair(i):
            return acc[:, 2 * i:2 * i + 2, :]

        def flat(i):
            return pair(i).rearrange("p b c -> p (b c)")

        x_dram = scratch("x_dram", [SEQ, D], F32)
        qkA = scratch("qkA", [HEADS, 2, 2, HD, SEQ], F32)
        qB = scratch("qB", [HEADS, 2, HD, SEQ], F32)
        kB = scratch("kB", [KV_HEADS, 2, HD, SEQ], F32)
        vA = scratch("vA", [HEADS, P, 2, ST, HD], F32)
        vB = scratch("vB", [KV_HEADS, P, 2, ST, HD], F32)
        ext_dram = scratch("ext_dram", [DEPTH * HEADS, EXT + 1], F32)
        bias_dram = scratch("bias_dram", [DEPTH * HEADS, P, SW], F32)

        table_in = sem("table_in")
        const_in = sem("const_in")
        ext_ready = sem("ext_ready")
        ext_out = sem("ext_out")
        bias_out = sem("bias_out")
        ident_s = sem("ident_s")
        tab = sem("tab")
        tab_act = sem("tab_act")
        x_in = sem("x_in")
        x_saved = sem("x_saved")
        x_back = sem("x_back")
        raw_in = [sem(f"raw_in{i}") for i in range(RAW)]
        split_hi = sem("split_hi")
        split = sem("split")
        sq_done = sem("sq_done")
        ms_done = sem("ms_done")
        rt_done = sem("rt_done")
        rs_done = sem("rs_done")
        xs_done = sem("xs_done")
        ht_ps = sem("ht_ps")
        ht_hi = sem("ht_hi")
        ht_lo = sem("ht_lo")
        u_done = sem("u_done")
        rope_m = sem("rope_m")
        rope_o = sem("rope_o")
        rt_ps = sem("rt_ps")
        st_hi = sem("st_hi")
        st_lo = sem("st_lo")
        stored = [sem(f"stored{i}") for i in range(2)]
        filled = sem("filled")
        at_set = sem("at_set")
        unit_in = [sem(f"unit_in{i}") for i in range(2)]
        qk_done = sem("qk_done")
        sk_done = sem("sk_done")
        mx_done = sem("mx_done")
        ex_done = sem("ex_done")
        ri_done = sem("ri_done")
        pr_done = sem("pr_done")
        tr_done = sem("tr_done")
        ph_done = sem("ph_done")
        pl_done = sem("pl_done")
        av_done = sem("av_done")
        y_done = sem("y_done")
        z_done = sem("z_done")
        silu_done = sem("silu_done")
        zy_done = sem("zy_done")
        yg_h = sem("yg_h")
        yg_l = sem("yg_l")
        g_done = sem("g_done")
        yo_done = sem("yo_done")
        sig_done = sem("sig_done")
        mm_done = sem("mm_done")
        mg_h = sem("mg_h")
        mg_l = sem("mg_l")
        o_done = sem("o_done")
        x_new = sem("x_new")
        gain_in = sem("gain_in")
        fin_sq = sem("fin_sq")
        fin_ms = sem("fin_ms")
        fin_y = sem("fin_y")
        out_s = sem("out_s")

        PAIRS = TILES // 2
        ORDER = {"A": 0, "B": 1}
        LEFT = {"A": A_LEFT, "B": B_LEFT}
        WIDE = {"A": SW, "B": 2 * P}
        SB = {"A": 4, "B": 8}
        TR_BANKS = {"A": (4, 5, 6), "B": (2, 3, 4, 5)}
        AV_BANKS = {"A": (7,), "B": (6, 7)}

        def tile_no(l, which, it, t):
            return (l * 2 + ORDER[which]) * HP * TILES + it * TILES + t

        def pair_no(l, which, it, a):
            return (l * 2 + ORDER[which]) * HP * PAIRS + it * PAIRS + a

        def unit_total(l, which, it):
            n_q, n_kv, n_bias = 16, 16 * 4, 16 * 2
            n_a = n_q + n_kv + n_bias
            before = l * (HP * (n_a + n_q) + KV_HEADS * n_kv)
            if which == "A":
                return before + (it + 1) * n_a
            return before + HP * n_a + (it + 1) * n_q + (it // 2 + 1) * n_kv

        def stored_after(l, s, more=0):
            n = [8] * (UB - 2) + [6] * 2 + [8] * UV + [2] * UT
            return 16 * (l * sum(n[0::2]) + sum(n[s % 2:s + 1:2]) + 2 * more)

        def blocks(which, m):
            lo = max(0, m - LEFT[which])
            return lo, m - lo + 1

        def scores(which, t):
            m = t % ST
            nb = blocks(which, m)[1]
            wide = WIDE[which]
            return s_buf[which][t % SB[which]], slice(wide - nb * P, wide), nb

        def groups(which, t):
            n = first_group(which, t)
            nb = blocks(which, t % ST)[1]
            parts = [(0, nb)] if nb <= 4 else [(0, nb - nb // 2), (nb - nb // 2, nb // 2)]
            banks = TR_BANKS[which]
            return [(n + i, banks[(n + i) % len(banks)], a, k) for i, (a, k) in enumerate(parts)]

        def first_group(which, t):
            return sum(1 if blocks(which, j % ST)[1] <= 4 else 2 for j in range(t))

        GROUPS = {w: first_group(w, TILES) for w in "AB"}
        assert all(GROUPS[w] % len(TR_BANKS[w]) == 0 for w in "AB")

        def group_no(l, which, it, g):
            before = l * HP * (GROUPS["A"] + GROUPS["B"])
            return before + (it * GROUPS["A"] + g if which == "A" else HP * GROUPS["A"] + it * GROUPS["B"] + g)

        def slots_of(which, t, a, k):
            m = t % ST
            s0 = blocks(which, m)[0] - (2 * (m // 2) - LEFT[which]) + a
            return (slice(None), (t // 2) % PT[which], slice(s0, s0 + k), slice(m % 2 * P, m % 2 * P + P))

        def qk_dst(which, t):
            return flat(t % 2) if which == "A" else acc[:, t % 2, :]

        def is_first(it):
            return isinstance(it, int) and it == 0

        def used(l, n):
            if n < W_T:
                return u_done, l * NU + 2 * (n // 2) + 2
            if n < W_Z:
                return u_done, l * NU + UB + UV + (n - W_T) + 1
            if n < W_M:
                return z_done, l * N_Z + (n - W_Z) + 1
            if n < W_O:
                i, d = divmod(n - W_M, 3)
                return (yo_done, l * 2 * KC + 2 * i + 2) if d == 2 else (g_done, l * 2 * KC + 2 * i + d + 1)
            return o_done, l * KC + 2 * ((n - W_O) // 2) + 2 + O_DONE0

        held = {e: sem(f"held_{e}") for e in ("sp", "pool", "pe", "dve")}

        def hold(name, eng, s, value):
            eng.wait_ge(s, value)
            eng.sem_inc(held[name], 1)

        block = ctx.enter_context(nc.Block())

        @block.sync
        def _(sp):
            w_in_v = w_in.rearrange("l (k p) c -> p (l k) c", p=P)
            w_o_v = w_out.rearrange("l (k p) c -> p (l k) c", p=P)
            w_a_v = w_a_out.rearrange("l (k p) c -> p (l k) c", p=P)
            w_b_v = w_b_out.rearrange("l (k p) c -> p (l k) c", p=P)
            x_v = x.rearrange("b (m p) c -> p (b m) c", p=P)
            xd_v = x_dram.rearrange("(m p) c -> p m c", p=P)
            NH = KC // 2

            for m in range(ST):
                sp.dma_start(xt[:, m, :], x_v[:, m, :]).then_inc(x_in, 16)

            def load(l, n, slot, parts):
                hold("sp", sp, split, l * NW + n - RAW + 1 + SPLIT0)
                for h, src in enumerate(parts):
                    sp.dma_start(w_raw[:, slot, h * NH:(h + 1) * NH], src).then_inc(raw_in[slot], 16)

            def full(view, l, c0):
                return [view[:, ds(l * KC + h * NH, NH), ds(c0, P)] for h in range(2)]

            def load_in(l, n, c0):
                load(l, n, n % RAW, full(w_in_v, l, c0))

            def heads(l, which, it, u):
                s = unit_in[u]

                def load_head(dst, src):
                    sp.dma_start(dst.bitcast(F32), src).then_inc(s, 16)

                if which == "A":
                    one = qkA[ds(2 * it + u, 1)].rearrange("a b h p s -> (a b) h p s")
                    q, k, v = one[0], one[1], vA[ds(2 * it + u, 1)].rearrange("a p h m c -> (a p) h m c")
                else:
                    g = it // 2
                    q, k, v = qB[2 * it + u], kB[g], vB[g]
                load_head(q_st[u][:, :], q)
                if which == "A" or it % 2 == 0:
                    load_head(k_st[u][:, :], k)
                    for part in range(2):
                        load_head(k_sw[u][part * HD:part * HD + HD, :], k[1 - part])
                    load_head(v_st[u][:, :, :, :], v)
                if which == "A":
                    row = l * HEADS + 2 * it + u
                    for rows, cols in ((slice(0, CHUNK), slice(0, SW - CHUNK)),
                                       (slice(CHUNK, P), slice(CHUNK, SW))):
                        src = bias_dram[ds(row, 1), rows, cols].rearrange("a p c -> (a p) c")
                        sp.dma_start(bias["A"][u][rows, cols], src).then_inc(s, 16)

            def next_heads(l, which, it):
                for u in range(2):
                    hold("sp", sp, av_done, pair_no(l, which, it - 1, 4 * (u + 1)))
                    heads(l, which, it, u)

            sp.wait_ge(ext_ready, 2)
            sp.dma_start(ext_dram[:, 0:EXT], ext[:, :]).then_inc(ext_out, 16)

            sp.wait_ge(ext_out, 16)
            for r in range(DEPTH):
                src = bass.AP(ext_dram.tensor, r * HEADS * (EXT + 1) + P - 1, [[EXT + 1, HEADS], [-1, P], [1, SW]])
                sp.dma_start(bias_dram[r * HEADS:(r + 1) * HEADS], src).then_inc(bias_out, 16)

            with sp.Fori(0, DEPTH) as l:
                for n in range(2):
                    load_in(l, n, COL["qB"] + P * n)
                sp.wait_ge(x_in, 16 * ST)
                sp.wait_ge(x_new, l * KC + X_NEW0)
                for m in range(ST):
                    sp.dma_start(xd_v[:, m, :], xt[:, m, :]).then_inc(x_saved, 16)
                for n in range(2, N_B):
                    load_in(l, n, COL["qB"] + P * n)
                for n in range(N_V):
                    load_in(l, W_V + n, COL["vA"] + P * n)
                for n in range(N_T):
                    load_in(l, W_T + n, (n % 2) * WIDTH + P * (n // 2))
                for n in range(2):
                    load_in(l, W_Z + n, COL["zA"] + P * n)
                sp.wait_ge(x_saved, 16 * ST * (l + 1))
                for s in (UB + UV, UB + UV + 1):
                    sp.wait_ge(stored[s % 2], stored_after(l, s))
                sp.wait_ge(bias_out, 16 * DEPTH)
                for u in range(2):
                    heads(l, "A", 0, u)
                for n in range(2, 4):
                    load_in(l, W_Z + n, COL["zA"] + P * n)
                for s in (NU - 2, NU - 1):
                    hold("sp", sp, stored[s % 2], stored_after(l, s))
                with sp.Fori(1, HP) as it:
                    next_heads(l, "A", it)
                for u in range(2):
                    hold("sp", sp, av_done, pair_no(l, "A", HP - 1, 4 * (u + 1)))
                    heads(l, "B", 0, u)
                for it in range(1, HP):
                    next_heads(l, "B", it)
                for n in range(4, N_Z):
                    load_in(l, W_Z + n, COL["zB"] + P * (n - 4))
                with sp.Fori(0, KC // 4) as ib:
                    for j in range(4):
                        n = W_M + 3 * (4 * ib + j)
                        c0 = (4 * ib + j) * P
                        slot = (W_M + 3 * j) % RAW
                        load(l, n, slot, full(w_in_v, l, COL["gA"] + c0))
                        load(l, n + 1, 1 - slot, full(w_in_v, l, COL["gB"] + c0))
                        load(l, n + 2, slot, [v[:, ds(l * NH, NH), ds(c0, P)] for v in (w_a_v, w_b_v)])
                for n in range(2):
                    load(l, W_O + n, (W_O + n) % RAW, full(w_o_v, l, P * n))
                sp.wait_ge(yo_done, 2 * KC * (l + 1))
                for m in range(ST):
                    sp.dma_start(xt[:, m, :], xd_v[:, m, :]).then_inc(x_back, 16)
                for n in range(2, N_O):
                    load(l, W_O + n, (W_O + n) % RAW, full(w_o_v, l, P * n))
            sp.wait_ge(mg_l, DEPTH * KC)
            sp.dma_start(g_row[:, :], final_g.rearrange("(a c) -> a c", a=1).to_broadcast([P, D])
                         ).then_inc(gain_in, 16)
            o_v = out.rearrange("b (m p) c -> p (b m) c", p=P)
            for m in range(ST):
                sp.wait_ge(fin_y, m + 1)
                sp.dma_start(o_v[:, m, :], xs[:, m, :]).then_inc(out_s, 16)
            sp.wait_ge(out_s, 16 * ST)

        @block.gpsimd
        def _(pool):
            for s, v in ((split, SPLIT0), (x_new, X_NEW0), (o_done, O_DONE0), (zy_done, ZY0),
                         (silu_done, SILU0), (sig_done, SIG0), (mm_done, MM0)):
                pool.sem_inc(s, v)
            pool.memset(ident[:, :], 0.0).then_inc(ident_s, 1)
            pool.wait_ge(ident_s, 1)
            pool.affine_select(out=ident[:, :], in_=ident[:, :], compare_op=ALU.not_equal, fill=1.0,
                               base=0, pattern=[[-1, P]], channel_multiplier=1).then_inc(ident_s, 1)

            def split_block(l, n):
                raw, hi, lo = w_raw[:, n % RAW], w_hi[:, n % SLOTS], w_lo[:, n % SLOTS]
                pool.wait_ge(raw_in[n % RAW], 32 * (l * (NW // 2) + n // 2 + 1))
                if n < 2:
                    pool.wait_ge(o_done, l * KC + O_DONE0)
                elif n >= SLOTS:
                    pool.wait_ge(*used(l, n - SLOTS))
                pool.sem_inc(held["pool"], 1)
                pool.tensor_scalar(hi, raw, 1.0, 1.0, ALU.mult, ALU.mult).then_inc(split_hi, 1)
                pool.wait_ge(split_hi, l * NW + n + 1)
                pool.tensor_tensor(lo, raw, hi.bitcast(F32), ALU.subtract).then_inc(split, 1)

            def probs(l, which, it, t):
                buf, cols, _ = scores(which, t)
                i = t % SB[which]
                hold("pool", pool, ri_done, tile_no(l, which, it, t) + 1)
                pool.tensor_scalar(buf[:, cols], buf[:, cols], rinv[:, i:i + 1], 1.0,
                                   ALU.mult, ALU.mult).then_inc(pr_done, 1)

            def fill(l, n, rows, cols, buf, value):
                pool.memset(buf[rows, cols], value).then_inc(filled, 1)
                hold("pool", pool, filled, l * FILLS + n + 1)

            def zeros(l, n, which):
                for t in (pt_hi[which], pt_lo[which]):
                    for b in range(PT[which]):
                        pool.memset(t[:, b, LEFT[which] + 1, 0:P].bitcast(F32), 0.0)
                        last = pool.memset(t[:, b, 0, P:2 * P].bitcast(F32), 0.0)
                last.then_inc(filled, 1)
                hold("pool", pool, filled, l * FILLS + n + 1)

            early, late, every = slice(0, CHUNK), slice(CHUNK, P), slice(0, P)
            first, last = slice(0, CHUNK), slice(SW - CHUNK, SW)
            fills_a = [(rows, cols, b, -BIG) for b in bias["A"] for rows, cols in ((late, first), (early, last))]
            c4 = [slice(j * CHUNK, j * CHUNK + CHUNK) for j in range(4)]
            fills_b = [(every, c4[0], bias["B"][0], -BIG), (every, c4[2], bias["B"][0], 0.0),
                       (early, c4[1], bias["B"][0], 0.0), (late, c4[1], bias["B"][0], -BIG),
                       (early, c4[3], bias["B"][0], -BIG), (late, c4[3], bias["B"][0], 0.0)]
            FILLS = len(fills_a) + len(fills_b) + 2

            with pool.Fori(0, DEPTH) as l:
                for n in range(W_T + 2):
                    split_block(l, n)
                hold("pool", pool, st_lo, l * NU + UB)
                zeros(l, 0, "A")
                for n, f in enumerate(fills_a):
                    fill(l, 1 + n, *f)
                pool.sem_inc(at_set, 1)
                for n in range(W_T + 2, W_Z + 2):
                    split_block(l, n)
                pipeline(pool, [(0, lambda it, t: probs(l, "A", it, t))], TILES, HP)
                hold("pool", pool, av_done, pair_no(l, "B", 0, 0))
                zeros(l, 1 + len(fills_a), "B")
                for n, f in enumerate(fills_b):
                    fill(l, 2 + len(fills_a) + n, *f)
                pool.sem_inc(at_set, 1)
                pipeline(pool, [(0, lambda it, t: probs(l, "B", it, t))], TILES, HP)
                for n in range(W_Z + 2, NW):
                    split_block(l, n)

        @block.tensor
        def _(pe):
            def mm3(dst, stat, mov, first, last):
                pe.matmul(dst, stat[0], mov[0], start=first, stop=False)
                pe.matmul(dst, stat[0], mov[1], start=False, stop=False)
                return pe.matmul(dst, stat[1], mov[0], start=False, stop=last)

            def t_unit(c, chunks, mov, at_chunk, banks):
                for h in range(2):
                    cols = slice(h * 512, h * 512 + 512)
                    for i, k in enumerate(chunks):
                        mm = mm3(pair(banks)[:, h, :],
                                 [w[:, c % SLOTS, k, :] for w in (w_hi, w_lo)],
                                 [t[:, at_chunk + i, cols] for t in mov],
                                 i == 0, i == len(chunks) - 1)
                return mm

            def rows_unit(c, stat, half, banks):
                two = slice(c % SLOTS, c % SLOTS + 2)
                for j in range(4):
                    rows = slice((4 * half + j) * P, (4 * half + j) * P + P)
                    for k in range(KC):
                        mm = mm3(flat(banks)[:, 256 * j:256 * j + 256], [t[:, k, rows] for t in stat],
                                 [w[:, two, k, :] for w in (w_hi, w_lo)], k == 0, k == KC - 1)
                return mm

            hT = (hT_hi, hT_lo)

            def rotated(l, u):
                pe.wait_ge(rope_o, l * 2 * UB + 2 * u + 2)
                if u >= 2:
                    pe.wait_ge(st_lo, l * NU + u - 1)
                for cb in range(2 if u < UB - 2 else 1):
                    for j in range(4):
                        mm = pe.transpose(pair(2 + u % 2)[:, cb, j * P:j * P + P],
                                          rot[:, u % 2, j, cb * P:cb * P + P], ident[:, :])
                mm.then_inc(rt_ps, 1)

            def qk(l, which, it, t):
                u, m = divmod(t, ST)
                lo, nb = blocks(which, m)
                if m == 0:
                    pe.wait_ge(unit_in[u], unit_total(l, which, it))
                if not (is_first(it) and t < 2):
                    pe.wait_ge(mx_done, tile_no(l, which, it, t) - 1)
                w = max(nb, 2) * P
                for i, (a, b) in enumerate([(0, w)] if w <= 512 else [(0, w // 2), (w // 2, w)]):
                    dst = pair(t % 2)[:, i, 0:b - a] if which == "A" else acc[:, t % 2, 0:b - a]
                    keys = slice(lo * P + a, lo * P + b)
                    q = q_st[u][:, m * P:m * P + P]
                    pe.matmul(dst, q, k_st[u][:, keys], start=True, stop=False)
                    mm = pe.matmul(dst, q, k_sw[u][:, keys], start=False, stop=True)
                mm.then_inc(qk_done, 1)

            def tr(l, which, it, t):
                buf, cols, nb = scores(which, t)
                pe.wait_ge(pr_done, tile_no(l, which, it, t) + 1)
                for g, bank, first, k in groups(which, t):
                    if not (is_first(it) and g < len(TR_BANKS[which])):
                        pe.wait_ge(pl_done, group_no(l, which, it, g) - len(TR_BANKS[which]) + 1)
                    for i in range(k):
                        a = cols.start + (first + i) * P
                        mm = pe.transpose(acc[:, bank, i * P:i * P + P], buf[:, a:a + P], ident[:, :])
                    mm.then_inc(tr_done, 1)

            def av(l, which, it, t):
                if t % 2 == 0:
                    return
                u, m = divmod(t, ST)
                a = m // 2
                no = pair_no(l, which, it, t // 2)
                pe.wait_ge(pl_done, group_no(l, which, it, first_group(which, t + 1)))
                banks = AV_BANKS[which]
                if not (is_first(it) and t // 2 < len(banks)):
                    pe.wait_ge(y_done, no - len(banks) + 1)
                dst = acc[0:HD, banks[(t // 2) % len(banks)], 0:256]
                slots = range(max(0, LEFT[which] - 2 * a), LEFT[which] + 2)
                for i in slots:
                    j = 2 * a - LEFT[which] + i
                    mm = mm3(dst, [v_st[u][:, part, j, :] for part in range(2)],
                             [t_[:, (t // 2) % PT[which], i, :] for t_ in (pt_hi[which], pt_lo[which])],
                             i == slots[0], i == slots[-1])
                mm.then_inc(av_done, 1)

            def banks_left(l, which):
                pe.wait_ge(mx_done, tile_no(l, which, 0, 0))
                pe.wait_ge(pl_done, group_no(l, which, 0, 0))
                hold("pe", pe, y_done, pair_no(l, which, 0, 0))

            pe.wait_ge(ident_s, 2)
            with pe.Fori(0, DEPTH) as l:
                for h in range(2):
                    pe.wait_ge(xs_done, l * ST + 4 * h + 4)
                    for k in range(KC):
                        if h == 1:
                            pe.wait_ge(ht_lo, l * 2 * KC + k + 1)
                        for j in range(4):
                            mm = pe.transpose(acc[:, k, j * P:j * P + P],
                                              xs[:, 4 * h + j, k * P:k * P + P], ident[:, :])
                        mm.then_inc(ht_ps, 1)
                pe.wait_ge(ht_lo, (l + 1) * 2 * KC)
                for u in range(UB + UV):
                    if u % 2 == 0:
                        pe.wait_ge(split, l * NW + u + 2 + SPLIT0)
                    if u >= 2 and u < UB:
                        pe.wait_ge(rope_m, l * 2 * UB + 2 * (u - 2) + 2)
                    if u >= UB:
                        pe.wait_ge(st_lo, l * NU + u - 1)
                    rows_unit(u - u % 2, hT, u % 2, u % 2).then_inc(u_done, 1)
                    if 1 <= u <= UB:
                        rotated(l, u - 1)
                with pe.Fori(0, N_T // 4) as ib:
                    for j in range(4):
                        pe.wait_ge(split, l * NW + W_T + 4 * ib + j + 1 + SPLIT0)
                        pe.wait_ge(st_lo, l * NU + UB + UV + 4 * ib + j - 1)
                        t_unit(W_T + j, range(KC), hT, 0, j % 2).then_inc(u_done, 1)
                pe.wait_ge(st_lo, (l + 1) * NU)
                pe.wait_ge(at_set, 2 * l + 1)
                for which in "AB":
                    if which == "B":
                        pe.wait_ge(at_set, 2 * l + 2)
                        banks_left(l, "B")
                    pipeline(pe, [(LAG[which]["qk"], lambda it, t: qk(l, which, it, t)),
                                  (LAG[which]["tr"], lambda it, t: tr(l, which, it, t)),
                                  (LAG[which]["av"], lambda it, t: av(l, which, it, t))], TILES, HP)
                banks_left(l + 1, "A")
                with pe.Fori(0, N_Z // 4) as ib:
                    for j in range(4):
                        b = 4 * ib + j
                        pe.wait_ge(split, l * NW + W_Z + b + 1 + SPLIT0)
                        pe.wait_ge(silu_done, l * N_Z + b - 1 + SILU0)
                        t_unit(W_Z + j, range(KC), hT, 0, j % 2).then_inc(z_done, 1)
                pe.wait_ge(silu_done, (l + 1) * N_Z + SILU0)
                pe.sem_inc(held["pe"], 1)
                with pe.Fori(0, KC // 4) as ib:
                    for j in range(4):
                        i = 4 * ib + j
                        c = W_M + 3 * j
                        for br in range(2):
                            pe.wait_ge(split, l * NW + W_M + 3 * i + br + 1 + SPLIT0)
                            pe.wait_ge(sig_done, l * 2 * KC + 2 * i + br - 1 + SIG0)
                            t_unit(c + br, range(KC), hT, 0, 2 * br).then_inc(g_done, 1)
                            if br == 0:
                                pe.wait_ge(split, l * NW + W_M + 3 * i + 3 + SPLIT0)
                                pe.wait_ge(yg_l, (l + 1) * N_Z)
                            pe.wait_ge(mm_done, l * 3 * KC + 3 * (i - 1) + br + 1 + MM0)
                            t_unit(c + 2, range(4 * br, 4 * br + 4), (yg_hi, yg_lo), 4 * br,
                                   2 * br + 1).then_inc(yo_done, 1)
                pe.wait_ge(mg_l, (l + 1) * KC)
                for f in range(N_O):
                    if f % 2 == 0:
                        pe.wait_ge(split, l * NW + W_O + f + 2 + SPLIT0)
                    if f >= 4:
                        pe.wait_ge(x_new, l * KC + f - 3 + X_NEW0)
                    rows_unit(W_O + f - f % 2, (mg_hi, mg_lo), f % 2, f % 4).then_inc(o_done, 1)

        @block.scalar
        def _(act):
            copy = ACT.Copy
            for dst, src in ((pos_i[:, :], positions.rearrange("b (m p) -> p (b m)", p=P)),
                             (freq[:, :], rope_freq.rearrange("(a c) -> a c", a=1).to_broadcast([P, HALF])),
                             (g_t, norm_g.rearrange("l (k p) -> p (l k)", p=P)),
                             (nsink, sinks.rearrange("l h -> (l h)").rearrange("(a c) -> a c", a=1)
                              .to_broadcast([P, DEPTH * HEADS]))):
                with nc.allow_non_contiguous_dma(reason="a few KB"):
                    act.dma_start(dst, src).then_inc(const_in, 16)
            act.dma_start(table[:, :], rel_bias.rearrange("l h r -> (l h) r")).then_inc(table_in, 16)
            act.wait_ge(tab, TAB_STEPS)
            act.activation(sin_t[:, :, :].rearrange("p m c -> p (m c)"), ang[:, 0, :], ACT.Sin).then_inc(tab_act, 1)
            act.activation(cos_t[:, :, :].rearrange("p m c -> p (m c)"), ang[:, 1, :], ACT.Sin).then_inc(tab_act, 1)
            act.wait_ge(ext_out, 16)

            def exps(l, which, it, t):
                buf, cols, _ = scores(which, t)
                i = t % SB[which]
                end = cols.stop + (1 if which == "B" else 0)
                act.wait_ge(mx_done, tile_no(l, which, it, t) + 1)
                act.activation(buf[:, cols.start:end], buf[:, cols.start:end], ACT.Exp,
                               bias=nmax[:, i:i + 1], scale=-1.0,
                               accum_out=esum[:, i:i + 1]).then_inc(ex_done, 1)

            def p_hi(l, which, it, t):
                if t % 2 == 0 and not (is_first(it) and t // 2 < PT[which]):
                    act.wait_ge(av_done, pair_no(l, which, it, t // 2) - PT[which] + 1)
                for g, bank, first, k in groups(which, t):
                    act.wait_ge(tr_done, group_no(l, which, it, g) + 1)
                    act.activation(pt_hi[which][slots_of(which, t, first, k)],
                                   acc[:, bank, 0:k * P].rearrange("p (n c) -> p n c", c=P),
                                   copy).then_inc(ph_done, 1)

            def y_out(l, which, it, t):
                if t % 2 == 0:
                    return
                u, m = divmod(t, ST)
                a = m // 2
                act.wait_ge(av_done, pair_no(l, which, it, t // 2) + 1)
                act.activation(y_raw[u * HD:u * HD + HD, ds(ORDER[which] * HP + it, 1), a * 256:a * 256 + 256]
                               .rearrange("p a c -> p (a c)"),
                               acc[0:HD, AV_BANKS[which][(t // 2) % len(AV_BANKS[which])], 0:256], copy).then_inc(y_done, 1)

            def stage(l, u, c, ib=0):
                act.wait_ge(st_lo, l * NU + u + 1)
                half, s = c % 2, stored[c % 2]
                rows, tiles = slice(512 * half, 512 * half + 512), slice(4 * half, 4 * half + 4)
                for i, st in enumerate((stage_hi, stage_lo)):
                    src = st[:, c % 2, :].bitcast(F32)
                    by_row = src.rearrange("p (m h c) -> p m h c", m=4, c=HD)
                    if c < UB - 2:
                        for j in range(4):
                            act.dma_start(qB[4 * (c // 2) + j, i, :, rows],
                                          src[j % 2 * HD:j % 2 * HD + HD, j // 2 * 512:j // 2 * 512 + 512]
                                          ).then_inc(s, 16)
                    elif c < UB:
                        act.dma_start(kB[:, i, :, rows], src[:, 0:512]).then_inc(s, 16)
                        by_row = src[:, 512:1024].rearrange("p (m h c) -> p m h c", m=4, c=HD)
                        for j in range(KV_HEADS):
                            act.dma_start(vB[j, :, i, tiles, :], by_row[:, :, j, :]).then_inc(s, 16)
                    elif c < UB + UV:
                        for j in range(4):
                            act.dma_start(vA[4 * ((c - UB) // 2) + j, :, i, tiles, :], by_row[:, :, j, :]
                                          ).then_inc(s, 16)
                    else:
                        t = c - UB - UV
                        act.dma_start(qkA[ds(4 * ib + t // 2 * 2, 2), t % 2, i], src).then_inc(s, 16)

            with act.Fori(0, DEPTH) as l:
                act.wait_ge(x_in, 16 * ST)
                act.wait_ge(x_new, l * KC + X_NEW0)
                for m in range(ST):
                    act.activation(xs[:, m, :], xt[:, m, :], ACT.Square,
                                   accum_out=ssq[:, m:m + 1]).then_inc(sq_done, 1)
                act.wait_ge(ms_done, l + 1)
                act.activation(rms, ssq, ACT.Sqrt).then_inc(rt_done, 1)
                for i in range(2 * KC):
                    h, k = divmod(i, KC)
                    act.wait_ge(ht_ps, l * 2 * KC + i + 1)
                    act.activation(hT_hi[:, k, h * 512:h * 512 + 512], acc[:, k, :], copy,
                                   scale=g_now[:, k:k + 1]).then_inc(ht_hi, 1)
                for u in range(UB + UV):
                    if u >= 2:
                        act.wait_ge(stored[u % 2], stored_after(l, u - 2))
                    if u < UB - 2:
                        act.wait_ge(rt_ps, l * UB + u + 1)
                        act.activation(stage_hi[:, u % 2, :], flat(2 + u % 2), copy).then_inc(st_hi, 1)
                    elif u < UB:
                        act.wait_ge(rt_ps, l * UB + u + 1)
                        act.activation(stage_hi[:, u % 2, 0:512], pair(2 + u % 2)[:, 0, :], copy)
                        act.activation(stage_hi[:, u % 2, 512:1024].rearrange("p (m c) -> p m c", m=4),
                                       flat(u % 2).rearrange("p (m c) -> p m c", m=4)[:, :, P:2 * P],
                                       copy).then_inc(st_hi, 1)
                    else:
                        act.wait_ge(u_done, l * NU + u + 1)
                        act.activation(stage_hi[:, u % 2, :], flat(u % 2), copy).then_inc(st_hi, 1)
                    stage(l, u, u)
                with act.Fori(0, N_T // 4) as ib:
                    for j in range(4):
                        c = UB + UV + j
                        act.wait_ge(stored[j % 2], stored_after(l, c - 2, 2 * ib))
                        act.wait_ge(u_done, l * NU + c + 4 * ib + 1)
                        act.activation(stage_hi[:, j % 2, :], flat(j % 2), copy).then_inc(st_hi, 1)
                        stage(l, c + 4 * ib, c, ib)
                for s in (NU - 2, NU - 1):
                    act.wait_ge(stored[s % 2], stored_after(l, s))
                for which in "AB":
                    act.wait_ge(at_set, 2 * l + 1 + ORDER[which])
                    pipeline(act, [(LAG[which]["hi"], lambda it, t: p_hi(l, which, it, t)),
                                   (LAG[which]["y"], lambda it, t: y_out(l, which, it, t)),
                                   (LAG[which]["ex"], lambda it, t: exps(l, which, it, t))], TILES, HP)
                def gated_hi(b):
                    act.wait_ge(zy_done, l * N_Z + b + 1 + ZY0)
                    act.activation(yg_hi[:, ds(b, 1), :].rearrange("p a c -> p (a c)"),
                                   y_raw[:, ds(b, 1), :].rearrange("p a c -> p (a c)"), copy).then_inc(yg_h, 1)

                with act.Fori(0, N_Z // 4) as ib:
                    for j in range(4):
                        b = 4 * ib + j
                        act.wait_ge(z_done, l * N_Z + b + 1)
                        act.wait_ge(zy_done, l * N_Z + b + ZY0)
                        act.activation(sg[:, :], flat(j % 2), ACT.Silu).then_inc(silu_done, 1)
                        gated_hi(b)
                with act.Fori(0, KC) as i:
                    for br in range(2):
                        act.wait_ge(g_done, l * 2 * KC + 2 * i + br + 1)
                        act.wait_ge(mm_done, l * 3 * KC + 3 * i + br + MM0)
                        act.activation(sg[:, :], flat(2 * br), ACT.Sigmoid).then_inc(sig_done, 1)
                act.wait_ge(g_done, (l + 1) * 2 * KC)
                with act.Fori(0, KC) as i:
                    act.wait_ge(mm_done, l * 3 * KC + 3 * i + 3 + MM0)
                    act.activation(mg_hi[:, ds(i, 1), :].rearrange("p a c -> p (a c)"),
                                   merged[:, ds(i, 1), :].rearrange("p a c -> p (a c)"), copy).then_inc(mg_h, 1)
            act.wait_ge(x_new, DEPTH * KC + X_NEW0)
            for m in range(ST):
                act.activation(xs[:, m, :], xt[:, m, :], ACT.Square,
                               accum_out=ssq[:, m:m + 1]).then_inc(fin_sq, 1)
            act.wait_ge(fin_ms, 1)
            act.activation(rms, ssq, ACT.Sqrt).then_inc(fin_ms, 1)

        @block.vector
        def _(dve):
            dve.wait_ge(table_in, 16)
            far = SW - CHUNK * 2 + P - 1 - A_MAX_REL
            dve.tensor_scalar(ext[:, 0:far], table[:, TW - 1:TW].to_broadcast([DEPTH * HEADS, far]),
                              1 / SCALE, None, ALU.mult).then_inc(ext_ready, 1)
            dve.tensor_scalar(ext[:, far:EXT], table[:, TW - 1:TW - 1 - (EXT - far):-1], 1 / SCALE, None,
                              ALU.mult).then_inc(ext_ready, 1)
            dve.wait_ge(const_in, 64)
            n = [0]

            def step(ins):
                n[0] += 1
                ins.then_inc(tab, 1)
                dve.wait_ge(tab, n[0])

            a0, a1 = ang[:, 0, :], ang[:, 1, :]
            tn, tn_i, wr = turns[:, 0, :], turns_i[:, 0, :], wrap[:, 0, :]
            step(dve.tensor_scalar(nsink, nsink, -1.0, None, ALU.mult))
            step(dve.tensor_copy(pos_f[:, :], pos_i[:, :]))
            step(dve.tensor_tensor(a0.rearrange("p (m c) -> p m c", m=ST),
                                   pos_f[:, :].unsqueeze(2).to_broadcast([P, ST, HALF]),
                                   freq[:, :].unsqueeze(1).to_broadcast([P, ST, HALF]), ALU.mult))
            step(dve.tensor_scalar(tn, a0, 1 / (2 * np.pi), None, ALU.mult))
            step(dve.tensor_copy(tn_i, tn))
            step(dve.tensor_copy(tn, tn_i))
            for part in PI2:
                step(dve.scalar_tensor_tensor(out=a0, in0=tn, scalar=-part, in1=a0, op0=ALU.mult, op1=ALU.add))
            for a, op, lim in ((a0, ALU.is_gt, np.pi), (a0, ALU.is_lt, -np.pi), (a1, ALU.is_gt, np.pi)):
                if a is a1:
                    step(dve.tensor_scalar(a1, a0, np.pi / 2, None, ALU.add))
                step(dve.tensor_scalar(wr, a, lim, -2 * lim, op, ALU.mult))
                step(dve.tensor_tensor(a, a, wr, ALU.add))
            step(dve.tensor_scalar(ang[:, :, :], ang[:, :, :], 3.1415925, -3.1415925, ALU.min, ALU.max))
            assert n[0] == TAB_STEPS

            def buffer_free(l, which, it, t):
                if not (is_first(it) and t < SB[which]):
                    before = first_group(which, (t - SB[which]) % TILES + 1) - (GROUPS[which] if t < SB[which] else 0)
                    dve.wait_ge(tr_done, group_no(l, which, it, before))

            def sinks_of(l, which, it, t):
                if which == "B":
                    buf, cols, _ = scores(which, t)
                    buffer_free(l, which, it, t)
                    dve.sem_inc(held["dve"], 1)
                    dve.tensor_copy(buf[:, cols.stop:cols.stop + 1],
                                    nsink[:, ds(l * HEADS + 2 * it + t // ST, 1)]).then_inc(sk_done, 1)

            def maxes(l, which, it, t):
                buf, cols, nb = scores(which, t)
                no = tile_no(l, which, it, t)
                i = t % SB[which]
                b = bias[which][t // ST]
                if which == "A":
                    buffer_free(l, which, it, t)
                    start = 3e38
                else:
                    dve.wait_ge(sk_done, (l * HP + it) * TILES + t + 1)
                    start = buf[:, cols.stop:cols.stop + 1]
                hold("dve", dve, qk_done, no + 1)
                out_, in1, in0 = buf[:, cols], b[:, cols], qk_dst(which, t)[:, 0:nb * P]
                if nb * P > 512:
                    out_, in1 = [v.rearrange("p (h c) -> p h c", h=2) for v in (out_, in1)]
                    in0 = pair(t % 2)[:, :, 0:nb * P // 2]
                dve.tensor_tensor_reduce(out_, in0, in1, -SCALE, start, ALU.add, ALU.min,
                                         nmax[:, i:i + 1]).then_inc(mx_done, 1)

            def recips(l, which, it, t):
                i = t % SB[which]
                dve.wait_ge(ex_done, tile_no(l, which, it, t) + 1)
                dve.reciprocal(rinv[:, i:i + 1], esum[:, i:i + 1]).then_inc(ri_done, 1)

            def p_lo(l, which, it, t):
                for g, bank, first, k in groups(which, t):
                    where = slots_of(which, t, first, k)
                    dve.wait_ge(ph_done, group_no(l, which, it, g) + 1)
                    dve.tensor_tensor(pt_lo[which][where], acc[:, bank, 0:k * P].rearrange("p (n c) -> p n c", c=P),
                                      pt_hi[which][where].bitcast(F32), ALU.subtract).then_inc(pl_done, 1)

            def rope(l, u):
                h = u % 2
                wide = 8 if u < UB - 2 else 4
                ps = flat(h).rearrange("p (m g c) -> p m g c", m=4, c=HALF)[:, :, 0:wide, :]
                dve.wait_ge(u_done, l * NU + u + 1)
                for dst, tb in ((r_cos, cos_t), (r_sin, sin_t)):
                    dve.tensor_tensor(dst[:, :, :].rearrange("p m (g c) -> p m g c", c=HALF)[:, :, 0:wide, :], ps,
                                      tb[:, 4 * h:4 * h + 4, :].unsqueeze(2).to_broadcast([P, 4, wide, HALF]),
                                      ALU.mult).then_inc(rope_m, 1)
                dve.wait_ge(rope_m, l * 2 * UB + 2 * u + 2)
                if u >= 2:
                    dve.wait_ge(rt_ps, l * UB + u - 1)
                c4, s4, r4 = [v.rearrange("p m (g t c) -> p m g t c", t=2, c=HALF)[:, :, 0:wide // 2]
                              for v in (r_cos[:, :, :], r_sin[:, :, :], rot[:, u % 2])]
                dve.tensor_tensor(r4[:, :, :, 0], c4[:, :, :, 0], s4[:, :, :, 1], ALU.subtract).then_inc(rope_o, 1)
                dve.tensor_tensor(r4[:, :, :, 1], c4[:, :, :, 1], s4[:, :, :, 0], ALU.add).then_inc(rope_o, 1)
                dve.wait_ge(rope_o, l * 2 * UB + 2 * u + 2)

            def lo_of(l, u, c):
                s = c % 2
                dve.wait_ge(st_hi, l * NU + u + 1)
                hi, lo = stage_hi[:, s, :].bitcast(F32), stage_lo[:, s, :]
                if c < UB - 2:
                    dve.tensor_tensor(lo, flat(2 + s), hi, ALU.subtract).then_inc(st_lo, 1)
                elif c < UB:
                    dve.tensor_tensor(lo[:, 0:512], pair(2 + s)[:, 0, :], hi[:, 0:512], ALU.subtract)
                    dve.tensor_tensor(lo[:, 512:1024].rearrange("p (m c) -> p m c", m=4),
                                      flat(s).rearrange("p (m c) -> p m c", m=4)[:, :, P:2 * P],
                                      hi[:, 512:1024].rearrange("p (m c) -> p m c", m=4),
                                      ALU.subtract).then_inc(st_lo, 1)
                else:
                    dve.tensor_tensor(lo, flat(s), hi, ALU.subtract).then_inc(st_lo, 1)

            def inverse_root(done, l):
                for i, ins in enumerate((
                        lambda: dve.reciprocal(rstd, rms),
                        lambda: dve.tensor_tensor(rsq, rstd, rstd, ALU.mult),
                        lambda: dve.tensor_tensor(rsq, rsq, ssq, ALU.mult),
                        lambda: dve.tensor_scalar(rsq, rsq, -0.5, 1.5, ALU.mult, ALU.add),
                        lambda: dve.tensor_tensor(rstd, rstd, rsq, ALU.mult))):
                    ins().then_inc(done, 1)
                    dve.wait_ge(done, 5 * l + i + 1)

            dve.wait_ge(tab_act, 2)
            with dve.Fori(0, DEPTH) as l:
                dve.tensor_copy(g_now, g_t.rearrange("p (l k) -> p l k", l=DEPTH)[:, ds(l, 1), :]
                                .rearrange("p a k -> p (a k)"))
                dve.wait_ge(sq_done, (l + 1) * ST)
                dve.tensor_scalar(ssq, ssq, 1 / D, EPS, ALU.mult, ALU.add).then_inc(ms_done, 1)
                dve.wait_ge(rt_done, l + 1)
                inverse_root(rs_done, l)
                for m in range(ST):
                    dve.tensor_scalar(xs[:, m, :], xt[:, m, :], rstd[:, m:m + 1], None,
                                      ALU.mult).then_inc(xs_done, 1)
                for i in range(2 * KC):
                    h, k = divmod(i, KC)
                    cols = slice(h * 512, h * 512 + 512)
                    dve.wait_ge(ht_hi, l * 2 * KC + i + 1)
                    dve.scalar_tensor_tensor(out=hT_lo[:, k, cols], in0=acc[:, k, :], scalar=g_now[:, k:k + 1],
                                             in1=hT_hi[:, k, cols].bitcast(F32), op0=ALU.mult,
                                             op1=ALU.subtract).then_inc(ht_lo, 1)
                for u in range(UB):
                    rope(l, u)
                    if u >= 1:
                        lo_of(l, u - 1, u - 1)
                for u in range(UB - 1, UB + UV):
                    lo_of(l, u, u)
                with dve.Fori(0, N_T // 4) as ib:
                    for j in range(4):
                        lo_of(l, UB + UV + 4 * ib + j, UB + UV + j)
                for which in "AB":
                    dve.wait_ge(at_set, 2 * l + 1 + ORDER[which])
                    if which == "B":
                        dve.wait_ge(tr_done, group_no(l, "B", 0, 0))
                    pipeline(dve, [(LAG[which]["mx"], lambda it, t: sinks_of(l, which, it, t)),
                                   (LAG[which]["lo"], lambda it, t: p_lo(l, which, it, t)),
                                   (LAG[which]["ri"], lambda it, t: recips(l, which, it, t)),
                                   (LAG[which]["mx"], lambda it, t: maxes(l, which, it, t))], TILES, HP)
                with dve.Fori(0, N_Z) as b:
                    y = y_raw[:, ds(b, 1), :].rearrange("p a c -> p (a c)")
                    dve.wait_ge(silu_done, l * N_Z + b + 1 + SILU0)
                    dve.wait_ge(y_done, pair_no(l + 1, "A", 0, 0))
                    dve.tensor_tensor(y, y, sg[:, :], ALU.mult).then_inc(zy_done, 1)
                    dve.wait_ge(yg_h, l * N_Z + b + 1)
                    dve.tensor_tensor(yg_lo[:, ds(b, 1), :].rearrange("p a c -> p (a c)"), y,
                                      yg_hi[:, ds(b, 1), :].rearrange("p a c -> p (a c)").bitcast(F32),
                                      ALU.subtract).then_inc(yg_l, 1)
                with dve.Fori(0, KC) as i:
                    mg = merged[:, ds(i, 1), :].rearrange("p a c -> p (a c)")
                    base_mm = l * 3 * KC + 3 * i + MM0
                    for br, dst in enumerate((mg, sg[:, :])):
                        dve.wait_ge(sig_done, l * 2 * KC + 2 * i + br + 1 + SIG0)
                        dve.wait_ge(yo_done, l * 2 * KC + 2 * i + br + 1)
                        dve.tensor_tensor(dst, flat(2 * br + 1), sg[:, :], ALU.mult).then_inc(mm_done, 1)
                    dve.wait_ge(mm_done, base_mm + 2)
                    dve.tensor_tensor(mg, mg, sg[:, :], ALU.add).then_inc(mm_done, 1)
                with dve.Fori(0, KC) as i:
                    dve.wait_ge(mg_h, l * KC + i + 1)
                    dve.tensor_tensor(mg_lo[:, ds(i, 1), :].rearrange("p a c -> p (a c)"),
                                      merged[:, ds(i, 1), :].rearrange("p a c -> p (a c)"),
                                      mg_hi[:, ds(i, 1), :].rearrange("p a c -> p (a c)").bitcast(F32),
                                      ALU.subtract).then_inc(mg_l, 1)
                dve.wait_ge(x_back, 16 * ST * (l + 1))
                for f in range(N_O):
                    c0, h = 256 * (f // 2), f % 2
                    dve.wait_ge(o_done, l * KC + f + 1 + O_DONE0)
                    xv = xt[:, 4 * h:4 * h + 4, c0:c0 + 256]
                    dve.tensor_tensor(xv, flat(f % 4).rearrange("p (m c) -> p m c", m=4), xv,
                                      ALU.add).then_inc(x_new, 1)
            dve.wait_ge(fin_sq, ST)
            dve.tensor_scalar(ssq, ssq, 1 / D, EPS, ALU.mult, ALU.add).then_inc(fin_ms, 1)
            dve.wait_ge(fin_ms, 2)
            inverse_root(rs_done, DEPTH)
            dve.wait_ge(gain_in, 16)
            for m in range(ST):
                dve.scalar_tensor_tensor(out=xs[:, m, :], in0=xt[:, m, :], scalar=rstd[:, m:m + 1],
                                         in1=g_row[:, :], op0=ALU.mult, op1=ALU.mult).then_inc(fin_y, 1)


_INS = ["x", "positions", "norm_g", "w_in", "rel_bias", "sinks", "w_a_out", "w_b_out", "w_out", "final_g"]


def kernel(**inputs):
    import concourse.bacc as _bacc
    from concourse.bass_utils import run_bass_kernel_spmd as _run

    nc = _bacc.Bacc("TRN2", target_bir_lowering=False, num_devices=1)
    arrays, args = {}, []
    values = [(name, np.ascontiguousarray(inputs[name])) for name in _INS]
    values.append(("rope_freq", (ROPE_THETA ** (-np.arange(HALF) / HALF)).astype(np.float32)))
    for name, a in values:
        arrays[f"in_{name}"] = a
        args.append(nc.dram_tensor(f"in_{name}", a.shape, mybir.dt.from_np(a.dtype), kind="ExternalInput").ap())
    out = nc.dram_tensor("out_0", (1, SEQ, D), F32, kind="ExternalOutput").ap()
    build(nc, *args, out)
    r = _run(nc, [arrays], core_ids=[0])
    return r.results[0]["out_0"]
```

```python
from contextlib import ExitStack

import concourse.bass as bass
import numpy as np
from concourse import mybir
from concourse.bass import ds

F32 = mybir.dt.float32
F32R = mybir.dt.float32r
I32 = mybir.dt.int32
ACT = mybir.ActivationFunctionType
ALU = mybir.AluOpType

P = 128
DEPTH = 2
SEQ = 1024
D = 1024
CHUNK = 64
HD = 64
HEADS = 8
A_LEFT = 4
B_LEFT = 1
A_MAX_REL = 256
WIDTH = HEADS * HD
KV_HEADS = 2
KVW = KV_HEADS * HD
D_IN = 4 * WIDTH + WIDTH + 2 * KVW + WIDTH + 2 * D
HALF = HD // 2
ROPE_THETA = 10000.0
EPS = 1e-6
SCALE = HD ** -0.5
BIG = 1e30

KC = D // P
ST = SEQ // P
HP = HEADS // 2
COL = dict(zip(("qA", "kA", "vA", "zA", "qB", "kB", "vB", "zB", "gA", "gB"),
               np.cumsum([0, WIDTH, WIDTH, WIDTH, WIDTH, WIDTH, KVW, KVW, WIDTH, D]).tolist()))

N_B = 6
N_V = 4
N_T = 8
N_Z = 8
N_M = 3 * KC
N_O = KC
W_B, W_V = 0, N_B
W_T = W_V + N_V
W_Z = W_T + N_T
W_M = W_Z + N_Z
W_O = W_M + N_M
NW = W_O + N_O
SLOTS = 4
RAW = 2

UB, UV, UT = 6, 4, 8
NU = UB + UV + UT
TILES = 2 * ST
SPLIT0, X_NEW0, O_DONE0, ZY0, SILU0, SIG0, MM0 = 2, 4, 1, 1, 2, 4, 6

TAB_STEPS = 17

PI2 = (6.25, 135 / 2 ** 12, 237 / 2 ** 20)
PI2 += (2 * np.pi - sum(PI2),)


STAGES = {
    "A": {"pe": (("qk", 0), ("tr", 3), ("av0", 5), ("av1", 5)),
          "act": (("hi", 3), ("y", 6), ("exp", 0)),
          "dve": (("lo", 4), ("mx", 0), ("ri", 1), ("ya", 7)),
          "pool": (("pr", 0),)},
    "B": {"pe": (("qk", 0), ("tr", 4), ("av0", 6), ("av1", 6)),
          "act": (("hi", 4), ("y", 7), ("exp", 0)),
          "dve": (("sk", 0), ("lo", 5), ("mx", 0), ("ri", 1)),
          "pool": (("pr", 0),)}}


def pipeline(eng, name, l, which, stages):
    order = STAGES[which][name]
    for s in range(TILES):
        for stage, lag in order:
            if s >= lag:
                stages[stage](l, which, 0, s - lag)
    with eng.Fori(1, HP) as it:
        for s in range(TILES):
            for stage, lag in order:
                if s >= lag:
                    stages[stage](l, which, it, s - lag)
                else:
                    stages[stage](l, which, it - 1, s - lag + TILES)
    for s in range(TILES, TILES + max(lag for _, lag in order)):
        for stage, lag in order:
            if s - lag < TILES:
                stages[stage](l, which, HP - 1, s - lag)


def build(nc, x, positions, norm_g, w_in, rel_bias, sinks, w_a_out, w_b_out, w_out, final_g,
          rope_freq, out):
    ctx = ExitStack()
    with ctx:
        base = (nc.sbuf_base + 1023) // 1024 * 1024 - 512

        def at(name, shape, dt, kb):
            return nc.alloc_sbuf_tensor_at(name, shape, dt, offset=base + int(kb * 1024))

        def sem(name):
            return ctx.enter_context(nc.semaphore(name))

        def scratch(name, shape, dt):
            return nc.dram_tensor(name, shape, dt, kind="Internal").ap()

        hT_hi = at("hT_hi", [P, KC, SEQ], F32R, 0)
        hT_lo = at("hT_lo", [P, KC, SEQ], F32R, 32)
        mg_hi = at("mg_hi", [P, KC, SEQ], F32R, 0)
        mg_lo = at("mg_lo", [P, KC, SEQ], F32R, 32)
        xt = at("xt", [P, ST, D], F32, 64)
        xs = at("xs", [P, ST, D], F32, 96)
        yg_hi = at("yg_hi", [P, KC, SEQ], F32R, 64)
        yg_lo = at("yg_lo", [P, KC, SEQ], F32R, 96)
        q_st = [at(f"q_st{u}", [P, SEQ], F32R, 64 + 16 * u) for u in range(2)]
        k_st = [at(f"k_st{u}", [P, SEQ], F32R, 68 + 16 * u) for u in range(2)]
        k_sw = [at(f"k_sw{u}", [P, SEQ], F32R, 72 + 16 * u) for u in range(2)]
        v_st = [at(f"v_st{u}", [P, ST, 2, HD], F32R, 76 + 16 * u) for u in range(2)]
        PT = {"A": 2, "B": 4}
        pt_hi = {"A": at("ptA_hi", [P, PT["A"], A_LEFT + 2, 256], F32R, 96),
                 "B": at("ptB_hi", [P, PT["B"], B_LEFT + 2, 256], F32R, 96)}
        pt_lo = {"A": at("ptA_lo", [P, PT["A"], A_LEFT + 2, 256], F32R, 108),
                 "B": at("ptB_lo", [P, PT["B"], B_LEFT + 2, 256], F32R, 108)}
        SW = (A_LEFT + 1) * P
        s_at = [120, 122.625, 125.25, 184, 192, 194.625, 197.25, 200]
        s_buf = {"A": [at(f"sA{i}", [P, SW + 8], F32, kb) for i, kb in enumerate(s_at)],
                 "B": [at(f"sB{i}", [P, 2 * P + 8], F32, kb) for i, kb in
                       enumerate([120 + 33 / 32 * i for i in range(5)] + [200 + 33 / 32 * i for i in range(3)])]}
        bias = {"A": [at(f"biasA{u}", [P, SW], F32, 187 + 2.5 * u) for u in range(2)],
                "B": [at("maskB", [P, 2 * P], F32, 125.5)] * 2}
        w_hi = at("w_hi", [P, SLOTS, KC, P], F32R, 128)
        w_lo = at("w_lo", [P, SLOTS, KC, P], F32R, 144)
        w_raw = at("w_raw", [P, RAW, KC, P], F32, 160)
        stage_hi = at("stage_hi", [P, 2, SEQ], F32R, 168)
        stage_lo = at("stage_lo", [P, 2, SEQ], F32R, 176)
        r_cos = at("r_cos", [P, 4, 256], F32, 184)
        r_sin = at("r_sin", [P, 4, 256], F32, 188)
        rot = at("rot", [P, 2, 4, 256], F32, 192)
        y_raw = at("y_raw", [P, 2 * HP, SEQ], F32, 168)
        merged = at("merged", [P, KC, SEQ], F32, 168)
        sg = at("sg", [P, SEQ], F32, 200)
        cos_t = at("cos_t", [P, ST, HALF], F32, 204)
        sin_t = at("sin_t", [P, ST, HALF], F32, 205)
        ident = at("ident", [P, P], F32, 206)
        small = at("small", [P, 162], F32, 206.5)
        g_t = small[:, 0:16]
        g_now = small[:, 72:80]
        nsink = small[:, 16:32]
        ssq = small[:, 32:40]
        part_sq = small[:, 128:160].rearrange("p (m c) -> p m c", c=4)
        warm = small[:, 160:162]
        rms = small[:, 40:48]
        rstd = small[:, 48:56]
        nmax = small[:, 80:88]
        esum = small[:, 88:96]
        rinv = small[:, 96:104]
        rsq = small[:, 56:64]
        pos_i = at("pos_i", [P, ST], I32, 168)
        pos_f = at("pos_f", [P, ST], F32, 168.25)
        freq = at("freq", [P, HALF], F32, 168.5)
        ang = at("ang", [P, 2, ST * HALF], F32, 169)
        turns = at("turns", [P, 2, ST * HALF], F32, 171)
        turns_i = at("turns_i", [P, 2, ST * HALF], I32, 173)
        wrap = at("wrap", [P, 2, ST * HALF], F32, 175)
        TW = 2 * A_MAX_REL + 1
        table = at("table", [DEPTH * HEADS, TW], F32, 177)
        EXT = SW + P - 1
        ext = at("ext", [DEPTH * HEADS, EXT], F32, 180)
        g_row = at("g_row", [P, D], F32, 168)

        acc = ctx.enter_context(nc.psum_tensor("acc", [P, 8, 512], F32))

        def pair(i):
            return acc[:, 2 * i:2 * i + 2, :]

        def flat(i):
            return pair(i).rearrange("p b c -> p (b c)")

        x_dram = scratch("x_dram", [SEQ, D], F32)
        qkA = scratch("qkA", [HEADS, 2, 2, HD, SEQ], F32)
        qB = scratch("qB", [HEADS, 2, HD, SEQ], F32)
        kB = scratch("kB", [KV_HEADS, 2, HD, SEQ], F32)
        vA = scratch("vA", [HEADS, P, ST, 2, HD], F32)
        vB = scratch("vB", [KV_HEADS, P, ST, 2, HD], F32)
        ext_dram = scratch("ext_dram", [DEPTH * HEADS, EXT + 1], F32)
        ext_now = scratch("ext_now", [HEADS, EXT + 1], F32)
        bias_dram = scratch("bias_dram", [HEADS, P, SW], F32)

        table_in = sem("table_in")
        rope_in = sem("rope_in")
        const_in = sem("const_in")
        ext_ready = sem("ext_ready")
        ext_out = sem("ext_out")
        ext_set = sem("ext_set")
        bias_out = sem("bias_out")
        ident_s = sem("ident_s")
        tab = sem("tab")
        tab_act = sem("tab_act")
        x_in = [sem(f"x_in{m}") for m in range(ST)]
        x_saved = sem("x_saved")
        x_back = sem("x_back")
        raw_in = [sem(f"raw_in{i}") for i in range(RAW)]
        split_hi = sem("split_hi")
        split = sem("split")
        sq_done = sem("sq_done")
        ms_done = sem("ms_done")
        g_set = sem("g_set")
        no_sq = sem("no_sq")
        ms_in = sem("ms_in")
        rt_done = sem("rt_done")
        rs_done = sem("rs_done")
        xs_done = sem("xs_done")
        ht_ps = sem("ht_ps")
        ht_hi = sem("ht_hi")
        ht_lo = sem("ht_lo")
        u_done = sem("u_done")
        rope_m = sem("rope_m")
        rope_o = sem("rope_o")
        rt_ps = sem("rt_ps")
        st_hi = sem("st_hi")
        st_lo = sem("st_lo")
        vb_hi = sem("vb_hi")
        vb_lo = sem("vb_lo")
        stored = [sem(f"stored{i}") for i in range(2)]
        filled = sem("filled")
        mask_set = sem("mask_set")
        zero_set = sem("zero_set")
        unit_in = [sem(f"unit_in{i}") for i in range(2)]
        v_in = [sem(f"v_in{i}") for i in range(2)]
        qk_done = sem("qk_done")
        sk_done = sem("sk_done")
        mx_done = sem("mx_done")
        ex_done = sem("ex_done")
        ri_done = sem("ri_done")
        pr_done = sem("pr_done")
        tr_done = sem("tr_done")
        ph_done = sem("ph_done")
        pl_done = sem("pl_done")
        av_done = sem("av_done")
        y_half = sem("y_half")
        y_done = sem("y_done")
        z_done = sem("z_done")
        silu_done = sem("silu_done")
        zy_done = sem("zy_done")
        yg_h = sem("yg_h")
        yg_l = sem("yg_l")
        g_done = sem("g_done")
        yo_done = sem("yo_done")
        sig_done = sem("sig_done")
        mm_done = sem("mm_done")
        mg_h = sem("mg_h")
        mg_l = sem("mg_l")
        o_done = sem("o_done")
        x_new = sem("x_new")
        gain_in = sem("gain_in")
        fin_y = sem("fin_y")
        out_s = sem("out_s")

        PAIRS = TILES // 2
        ORDER = {"A": 0, "B": 1}
        LEFT = {"A": A_LEFT, "B": B_LEFT}
        WIDE = {"A": SW, "B": 2 * P}
        SB = {"A": 8, "B": 8}
        TR_BANKS = {"A": (4, 5), "B": (2, 3, 4, 5)}
        AV_BANKS = {"A": (6, 7), "B": (6, 7)}

        def tile_no(l, which, it, t):
            return (l * 2 + ORDER[which]) * HP * TILES + it * TILES + t

        def pair_no(l, which, it, a):
            return (l * 2 + ORDER[which]) * HP * PAIRS + it * PAIRS + a

        def unit_total(l, which, it):
            n_q, n_k, n_bias = 16, 16 * 3, 16 * 2
            n_a = n_q + n_k + n_bias
            before = l * (HP * (n_a + n_q) + KV_HEADS * n_k)
            if which == "A":
                return before + (it + 1) * n_a
            return before + HP * n_a + (it + 1) * n_q + (it // 2 + 1) * n_k

        def v_total(l, which, it):
            before = l * 16 * (HP + KV_HEADS)
            return before + 16 * (it + 1 if which == "A" else HP + it // 2 + 1)

        def stored_after(l, s, more=0):
            n = [8] * (UB - 2) + [6] * 2 + [8] * UV + [2] * UT
            return 16 * (l * sum(n[0::2]) + sum(n[s % 2:s + 1:2]) + 2 * more)

        def blocks(which, m):
            lo = max(0, m - LEFT[which])
            return lo, m - lo + 1

        def scores(which, t):
            m = t % ST
            nb = blocks(which, m)[1]
            wide = WIDE[which]
            return s_buf[which][t % SB[which]], slice(wide - nb * P, wide), nb

        def groups(which, t):
            n = first_group(which, t)
            nb = blocks(which, t % ST)[1]
            parts = [(0, nb)] if nb <= 4 else [(0, nb - nb // 2), (nb - nb // 2, nb // 2)]
            banks = TR_BANKS[which]
            return [(n + i, banks[(n + i) % len(banks)], a, k) for i, (a, k) in enumerate(parts)]

        def first_group(which, t):
            return sum(1 if blocks(which, j % ST)[1] <= 4 else 2 for j in range(t))

        GROUPS = {w: first_group(w, TILES) for w in "AB"}
        assert all(GROUPS[w] % len(TR_BANKS[w]) == 0 for w in "AB")

        def group_no(l, which, it, g):
            before = l * HP * (GROUPS["A"] + GROUPS["B"])
            return before + (it * GROUPS["A"] + g if which == "A" else HP * GROUPS["A"] + it * GROUPS["B"] + g)

        def slots_of(which, t, a, k):
            m = t % ST
            s0 = blocks(which, m)[0] - (2 * (m // 2) - LEFT[which]) + a
            return (slice(None), (t // 2) % PT[which], slice(s0, s0 + k), slice(m % 2 * P, m % 2 * P + P))

        def mm_no(l, i, step):
            return l * 6 * KC + 6 * i + ("A0", "A1", "B0", "S0", "B1", "S1").index(step) + 1 + MM0

        def y_rows(which, it, t):
            u, m = divmod(t, ST)
            return (y_raw[u * HD:u * HD + HD, ds(ORDER[which] * HP + it, 1), m // 2 * 256:m // 2 * 256 + 256]
                    .rearrange("p a c -> p (a c)"))

        def av_rows(which, t, part):
            banks = AV_BANKS[which]
            return acc[part * HD:part * HD + HD, banks[(t // 2) % len(banks)], 0:256]

        def qk_dst(which, t):
            return flat(t % 2) if which == "A" else acc[:, t % 2, :]

        def is_first(it):
            return isinstance(it, int) and it == 0

        def used(l, n):
            if n < W_T:
                return u_done, l * NU + 2 * (n // 2) + 2
            if n < W_Z:
                return u_done, l * NU + UB + UV + (n - W_T) + 1
            if n < W_M:
                return z_done, l * N_Z + (n - W_Z) + 1
            if n < W_O:
                i, d = divmod(n - W_M, 3)
                return (yo_done, l * 4 * KC + 4 * i + 4) if d == 2 else (g_done, l * 4 * KC + 4 * i + 2 * d + 2)
            return o_done, l * KC + 2 * ((n - W_O) // 2) + 2 + O_DONE0

        held = {e: sem(f"held_{e}") for e in ("sp", "pool", "pe", "dve")}

        def hold(name, eng, s, value):
            eng.wait_ge(s, value)
            eng.sem_inc(held[name], 1)

        block = ctx.enter_context(nc.Block())

        @block.sync
        def _(sp):
            w_in_v = w_in.rearrange("l (k p) c -> p (l k) c", p=P)
            w_o_v = w_out.rearrange("l (k p) c -> p (l k) c", p=P)
            w_a_v = w_a_out.rearrange("l (k p) c -> p (l k) c", p=P)
            w_b_v = w_b_out.rearrange("l (k p) c -> p (l k) c", p=P)
            x_v = x.rearrange("b (m p) c -> p (b m) c", p=P)
            xd_v = x_dram.rearrange("(m p) c -> p m c", p=P)
            NH = KC // 2

            for m in range(ST):
                sp.dma_start(xt[:, m, :], x_v[:, m, :]).then_inc(x_in[m], 16)

            def load(l, n, slot, parts):
                hold("sp", sp, split, l * NW + n - RAW + 1 + SPLIT0)
                for h, src in enumerate(parts):
                    sp.dma_start(w_raw[:, slot, h * NH:(h + 1) * NH], src).then_inc(raw_in[slot], 16)

            def full(view, l, c0):
                return [view[:, ds(l * KC + h * NH, NH), ds(c0, P)] for h in range(2)]

            def load_in(l, n, c0):
                load(l, n, n % RAW, full(w_in_v, l, c0))

            def head_qk(l, which, it, u):
                s = unit_in[u]
                if which == "A":
                    one = qkA[ds(2 * it + u, 1)].rearrange("a b h p s -> (a b) h p s")
                    q, k = one[0], one[1]
                else:
                    q, k = qB[2 * it + u], kB[it // 2]
                sp.dma_start(q_st[u][:, :].bitcast(F32), q).then_inc(s, 16)
                if which == "A" or it % 2 == 0:
                    sp.dma_start(k_st[u][:, :].bitcast(F32), k).then_inc(s, 16)
                    for part in range(2):
                        sp.dma_start(k_sw[u][part * HD:part * HD + HD, :].bitcast(F32), k[1 - part]).then_inc(s, 16)
                if which == "A":
                    row = 2 * it + u
                    for rows, cols in ((slice(0, CHUNK), slice(0, SW - CHUNK)),
                                       (slice(CHUNK, P), slice(CHUNK, SW))):
                        src = bias_dram[ds(row, 1), rows, cols].rearrange("a p c -> (a p) c")
                        sp.dma_start(bias["A"][u][rows, cols], src).then_inc(s, 16)

            def head_v(l, which, it, u):
                if which == "A":
                    v = vA[ds(2 * it + u, 1)].rearrange("a p m h c -> (a p) m h c")
                elif it % 2:
                    return
                else:
                    v = vB[it // 2]
                sp.dma_start(v_st[u][:, :, :, :].bitcast(F32), v).then_inc(v_in[u], 16)

            def next_heads(l, which, it, former, former_it):
                for u in range(2):
                    hold("sp", sp, mx_done, tile_no(l, former, former_it, ST * (u + 1)))
                    head_qk(l, which, it, u)
                    hold("sp", sp, av_done, pair_no(l, former, former_it, PAIRS // 2 * (u + 1)))
                    head_v(l, which, it, u)

            def expand_bias(l):
                sp.wait_ge(ext_out, 16)
                sp.dma_start(ext_now[:, 0:EXT], ext_dram[ds(l * HEADS, HEADS), 0:EXT]).then_inc(ext_set, 16)
                sp.wait_ge(ext_set, 16 * (l + 1))
                sp.dma_start(bias_dram, bass.AP(ext_now.tensor, P - 1, [[EXT + 1, HEADS], [-1, P], [1, SW]])
                             ).then_inc(bias_out, 16)

            with sp.Fori(0, DEPTH) as l:
                for n in range(2):
                    load_in(l, n, COL["qB"] + P * n)
                for s in x_in:
                    sp.wait_ge(s, 16)
                sp.wait_ge(x_new, l * KC + X_NEW0)
                for m in range(ST):
                    sp.dma_start(xd_v[:, m, :], xt[:, m, :]).then_inc(x_saved, 16)
                for n in range(2, N_B):
                    load_in(l, n, COL["qB"] + P * n)
                expand_bias(l)
                for n in range(N_V):
                    load_in(l, W_V + n, COL["vA"] + P * n)
                for n in range(N_T):
                    load_in(l, W_T + n, (n % 2) * WIDTH + P * (n // 2))
                for n in range(2):
                    load_in(l, W_Z + n, COL["zA"] + P * n)
                sp.wait_ge(x_saved, 16 * ST * (l + 1))
                for s in (UB + UV, UB + UV + 1):
                    sp.wait_ge(stored[s % 2], stored_after(l, s))
                sp.wait_ge(bias_out, 16 * (l + 1))
                for u in range(2):
                    head_qk(l, "A", 0, u)
                    head_v(l, "A", 0, u)
                for n in range(2, 4):
                    load_in(l, W_Z + n, COL["zA"] + P * n)
                for s in (NU - 2, NU - 1):
                    hold("sp", sp, stored[s % 2], stored_after(l, s))
                with sp.Fori(1, HP) as it:
                    next_heads(l, "A", it, "A", it - 1)
                next_heads(l, "B", 0, "A", HP - 1)
                for it in range(1, HP):
                    next_heads(l, "B", it, "B", it - 1)
                for n in range(4, N_Z):
                    load_in(l, W_Z + n, COL["zB"] + P * (n - 4))
                with sp.Fori(0, KC // 4) as ib:
                    for j in range(4):
                        n = W_M + 3 * (4 * ib + j)
                        c0 = (4 * ib + j) * P
                        slot = (W_M + 3 * j) % RAW
                        load(l, n, slot, full(w_in_v, l, COL["gA"] + c0))
                        load(l, n + 1, 1 - slot, full(w_in_v, l, COL["gB"] + c0))
                        load(l, n + 2, slot, [v[:, ds(l * NH, NH), ds(c0, P)] for v in (w_a_v, w_b_v)])
                for n in range(2):
                    load(l, W_O + n, (W_O + n) % RAW, full(w_o_v, l, P * n))
                sp.wait_ge(yo_done, 4 * KC * (l + 1))
                for m in range(ST):
                    sp.dma_start(xt[:, m, :], xd_v[:, m, :]).then_inc(x_back, 16)
                for n in range(2, N_O):
                    load(l, W_O + n, (W_O + n) % RAW, full(w_o_v, l, P * n))
            sp.wait_ge(mg_l, DEPTH * 2 * KC)
            sp.dma_start(g_row[:, :], final_g.rearrange("(a c) -> a c", a=1).to_broadcast([P, D])
                         ).then_inc(gain_in, 16)
            o_v = out.rearrange("b (m p) c -> p (b m) c", p=P)
            for m in range(ST):
                sp.wait_ge(fin_y, m + 1)
                sp.dma_start(o_v[:, m, :], xs[:, m, :]).then_inc(out_s, 16)
            sp.wait_ge(out_s, 16 * ST)

        @block.gpsimd
        def _(pool):
            for s, v in ((split, SPLIT0), (x_new, X_NEW0), (o_done, O_DONE0), (zy_done, ZY0),
                         (silu_done, SILU0), (sig_done, SIG0), (mm_done, MM0)):
                pool.sem_inc(s, v)
            pool.memset(small[:, 128:162], 0.0).then_inc(no_sq, 1)
            pool.memset(ident[:, :], 0.0).then_inc(ident_s, 1)
            pool.wait_ge(ident_s, 1)
            pool.affine_select(out=ident[:, :], in_=ident[:, :], compare_op=ALU.not_equal, fill=1.0,
                               base=0, pattern=[[-1, P]], channel_multiplier=1).then_inc(ident_s, 1)

            def split_block(l, n):
                raw, hi, lo = w_raw[:, n % RAW], w_hi[:, n % SLOTS], w_lo[:, n % SLOTS]
                pool.wait_ge(raw_in[n % RAW], 32 * (l * (NW // 2) + n // 2 + 1))
                if n < 2:
                    pool.wait_ge(o_done, l * KC + O_DONE0)
                elif n >= SLOTS:
                    pool.wait_ge(*used(l, n - SLOTS))
                pool.sem_inc(held["pool"], 1)
                pool.tensor_scalar(hi, raw, 1.0, 1.0, ALU.mult, ALU.mult).then_inc(split_hi, 1)
                pool.wait_ge(split_hi, l * NW + n + 1)
                pool.tensor_tensor(lo, raw, hi.bitcast(F32), ALU.subtract).then_inc(split, 1)

            def probs(l, which, it, t):
                buf, cols, _ = scores(which, t)
                i = t % SB[which]
                hold("pool", pool, ri_done, tile_no(l, which, it, t) + 1)
                pool.tensor_scalar(buf[:, cols], buf[:, cols], rinv[:, i:i + 1], 1.0,
                                   ALU.mult, ALU.mult).then_inc(pr_done, 1)

            def fill(l, n, rows, cols, buf, value):
                pool.memset(buf[rows, cols], value).then_inc(filled, 1)
                hold("pool", pool, filled, l * FILLS + n + 1)

            def zeros(l, n, which):
                for t in (pt_hi[which], pt_lo[which]):
                    for b in range(PT[which]):
                        pool.memset(t[:, b, LEFT[which] + 1, 0:P].bitcast(F32), 0.0)
                        last = pool.memset(t[:, b, 0, P:2 * P].bitcast(F32), 0.0)
                last.then_inc(filled, 1)
                hold("pool", pool, filled, l * FILLS + n + 1)

            early, late, every = slice(0, CHUNK), slice(CHUNK, P), slice(0, P)
            first, last = slice(0, CHUNK), slice(SW - CHUNK, SW)
            fills_a = [(rows, cols, b, -BIG) for b in bias["A"] for rows, cols in ((late, first), (early, last))]
            c4 = [slice(j * CHUNK, j * CHUNK + CHUNK) for j in range(4)]
            fills_b = [(every, c4[0], bias["B"][0], -BIG), (every, c4[2], bias["B"][0], 0.0),
                       (early, c4[1], bias["B"][0], 0.0), (late, c4[1], bias["B"][0], -BIG),
                       (early, c4[3], bias["B"][0], -BIG), (late, c4[3], bias["B"][0], 0.0)]
            FILLS = len(fills_a) + len(fills_b) + 2

            with pool.Fori(0, DEPTH) as l:
                for n in range(W_T + 2):
                    split_block(l, n)
                hold("pool", pool, st_lo, l * NU + UB)
                zeros(l, 0, "A")
                for n, f in enumerate(fills_a):
                    fill(l, 1 + n, *f)
                pool.sem_inc(mask_set, 1)
                pool.sem_inc(zero_set, 1)
                for n in range(W_T + 2, W_Z + 2):
                    split_block(l, n)
                pipeline(pool, "pool", l, "A", {"pr": probs})
                hold("pool", pool, tr_done, group_no(l, "B", 0, 0))
                for n, f in enumerate(fills_b):
                    fill(l, 1 + len(fills_a) + n, *f)
                pool.sem_inc(mask_set, 1)
                hold("pool", pool, av_done, pair_no(l, "B", 0, 0))
                zeros(l, 1 + len(fills_a) + len(fills_b), "B")
                pool.sem_inc(zero_set, 1)
                pipeline(pool, "pool", l, "B", {"pr": probs})
                for n in range(W_Z + 2, NW):
                    split_block(l, n)

        @block.tensor
        def _(pe):
            def mm3(dst, stat, mov, first, last):
                pe.matmul(dst, stat[0], mov[0], start=first, stop=False)
                pe.matmul(dst, stat[0], mov[1], start=False, stop=False)
                return pe.matmul(dst, stat[1], mov[0], start=False, stop=last)

            def t_half(c, chunks, mov, at_chunk, banks, h):
                cols = slice(h * 512, h * 512 + 512)
                for i, k in enumerate(chunks):
                    mm = mm3(pair(banks)[:, h, :], [w[:, c % SLOTS, k, :] for w in (w_hi, w_lo)],
                             [t[:, at_chunk + i, cols] for t in mov], i == 0, i == len(chunks) - 1)
                return mm

            def t_unit(*unit):
                t_half(*unit, 0)
                return t_half(*unit, 1)

            def rows_unit(c, stat, half, banks, ready=None, between=None):
                two = slice(c % SLOTS, c % SLOTS + 2)
                for j in range(4):
                    if between:
                        between(j)
                    rows = slice((4 * half + j) * P, (4 * half + j) * P + P)
                    for k in range(KC):
                        if ready and j == 0:
                            ready(k)
                        mm = mm3(flat(banks)[:, 256 * j:256 * j + 256], [t[:, k, rows] for t in stat],
                                 [w[:, two, k, :] for w in (w_hi, w_lo)], k == 0, k == KC - 1)
                return mm

            hT = (hT_hi, hT_lo)

            def rotated(l, u):
                pe.wait_ge(rope_o, l * 2 * UB + 2 * u + 2)
                if u >= 2:
                    pe.wait_ge(st_lo, l * NU + u - 1)
                for cb in range(2 if u < UB - 2 else 1):
                    for j in range(4):
                        mm = pe.transpose(pair(2 + u % 2)[:, cb, j * P:j * P + P],
                                          rot[:, u % 2, j, cb * P:cb * P + P], ident[:, :])
                mm.then_inc(rt_ps, 1)

            def qk(l, which, it, t):
                u, m = divmod(t, ST)
                lo, nb = blocks(which, m)
                if m == 0:
                    pe.wait_ge(unit_in[u], unit_total(l, which, it))
                if not (is_first(it) and t < 2):
                    pe.wait_ge(mx_done, tile_no(l, which, it, t) - 1)
                w = max(nb, 2) * P
                for i, (a, b) in enumerate([(0, w)] if w <= 512 else [(0, w // 2), (w // 2, w)]):
                    dst = pair(t % 2)[:, i, 0:b - a] if which == "A" else acc[:, t % 2, 0:b - a]
                    keys = slice(lo * P + a, lo * P + b)
                    q = q_st[u][:, m * P:m * P + P]
                    pe.matmul(dst, q, k_st[u][:, keys], start=True, stop=False)
                    mm = pe.matmul(dst, q, k_sw[u][:, keys], start=False, stop=True)
                mm.then_inc(qk_done, 1)

            def tr(l, which, it, t):
                buf, cols, nb = scores(which, t)
                if which == "A" and is_first(it) and t == 0:
                    pe.wait_ge(st_lo, (l + 1) * NU)
                if which == "B" and is_first(it) and t == 0:
                    pe.wait_ge(pl_done, group_no(l, "B", 0, 0))
                pe.wait_ge(pr_done, tile_no(l, which, it, t) + 1)
                for g, bank, first, k in groups(which, t):
                    if not (is_first(it) and g < len(TR_BANKS[which])):
                        pe.wait_ge(pl_done, group_no(l, which, it, g) - len(TR_BANKS[which]) + 1)
                    for i in range(k):
                        a = cols.start + (first + i) * P
                        mm = pe.transpose(acc[:, bank, i * P:i * P + P], buf[:, a:a + P], ident[:, :])
                    mm.then_inc(tr_done, 1)

            def av(l, which, it, t, half):
                if t % 2 == 0:
                    return
                u, m = divmod(t, ST)
                a = m // 2
                no = pair_no(l, which, it, t // 2)
                banks = AV_BANKS[which]
                if half == 0:
                    if m == 1:
                        pe.wait_ge(v_in[u], v_total(l, which, it))
                    if which == "B" and is_first(it) and t == 1:
                        pe.wait_ge(y_done, pair_no(l, "B", 0, 0))
                    pe.wait_ge(pl_done, group_no(l, which, it, first_group(which, t + 1)))
                    if not (is_first(it) and t // 2 < len(banks)):
                        pe.wait_ge(y_done, no - len(banks) + 1)
                dst = acc[:, banks[(t // 2) % len(banks)], 0:256]
                slots = list(range(max(0, LEFT[which] - 2 * a), LEFT[which] + 2))
                cut = (len(slots) + 1) // 2
                for i in (slots[cut:] if half else slots[:cut]):
                    j = 2 * a - LEFT[which] + i
                    p_hi_lo = [t_[:, (t // 2) % PT[which], i, :] for t_ in (pt_hi[which], pt_lo[which])]
                    if which == "B":
                        mm = mm3(dst[0:HD], [v_st[u][:, j, part, :] for part in range(2)], p_hi_lo,
                                 i == slots[0], i == slots[-1])
                        continue
                    v = v_st[u][:, j, :, :].rearrange("p h c -> p (h c)")
                    pe.matmul(dst, v, p_hi_lo[0], start=i == slots[0], stop=False)
                    mm = pe.matmul(dst, v, p_hi_lo[1], start=False, stop=i == slots[-1])
                if half == 1:
                    mm.then_inc(av_done, 1)

            def transposes(h, k, bank):
                for j in range(4):
                    mm = pe.transpose(acc[:, bank, j * P:j * P + P],
                                      xs[:, 4 * h + j, k * P:k * P + P], ident[:, :])
                mm.then_inc(ht_ps, 1)

            pe.wait_ge(ident_s, 2)
            with pe.Fori(0, DEPTH) as l:
                pe.wait_ge(xs_done, l * ST + 4)
                for k in range(KC):
                    pe.wait_ge(x_new, l * KC + k // 2 - 3 + X_NEW0)
                    transposes(0, k, k)
                def second_half(j):
                    if j < 2:
                        return
                    pe.wait_ge(xs_done, (l + 1) * ST)
                    for k in range(4 * j - 8, 4 * j - 4):
                        if k >= 4:
                            pe.wait_ge(ht_lo, l * 2 * KC + KC + k - 3)
                        transposes(1, k, 4 + k % 4)

                for u in range(UB + UV):
                    if u % 2 == 0:
                        pe.wait_ge(split, l * NW + u + 2 + SPLIT0)
                    if u >= 2 and u < UB:
                        pe.wait_ge(rope_m, l * 2 * UB + 2 * (u - 2) + 2)
                    if UB <= u < UB + 2:
                        pe.wait_ge(rope_m, l * 2 * UB + 2 * (u - 2) + 2)
                        pe.wait_ge(vb_lo, l * 2 + u - UB + 1)
                    if u >= UB + 2:
                        pe.wait_ge(st_lo, l * NU + u - 1)
                    rows_unit(u - u % 2, hT, u % 2, u % 2,
                              (lambda k: pe.wait_ge(ht_lo, l * 2 * KC + u * KC + k + 1)) if u < 2 else None,
                              second_half if u == 0 else None).then_inc(u_done, 1)
                    if 1 <= u <= UB:
                        rotated(l, u - 1)
                with pe.Fori(0, N_T // 4) as ib:
                    for j in range(4):
                        pe.wait_ge(split, l * NW + W_T + 4 * ib + j + 1 + SPLIT0)
                        pe.wait_ge(st_lo, l * NU + UB + UV + 4 * ib + j - 1)
                        t_unit(W_T + j, range(KC), hT, 0, 2 + j % 2).then_inc(u_done, 1)
                for which in "AB":
                    if which == "B":
                        hold("pe", pe, mx_done, tile_no(l, "B", 0, 0))
                    pipeline(pe, "pe", l, which, {"qk": qk, "tr": tr, "av0": lambda *n: av(*n, 0),
                                                        "av1": lambda *n: av(*n, 1)})
                hold("pe", pe, mx_done, tile_no(l + 1, "A", 0, 0))
                with pe.Fori(0, N_Z // 4) as ib:
                    for j in range(4):
                        b = 4 * ib + j
                        pe.wait_ge(split, l * NW + W_Z + b + 1 + SPLIT0)
                        pe.wait_ge(silu_done, l * N_Z + b - 1 + SILU0)
                        if j == 1:
                            pe.wait_ge(pl_done, group_no(l + 1, "A", 0, 0))
                        t_unit(W_Z + j, range(KC), hT, 0, j % 2).then_inc(z_done, 1)
                hold("pe", pe, silu_done, (l + 1) * N_Z - 1 + SILU0)
                with pe.Fori(0, KC // 4) as ib:
                    for j in range(4):
                        i = 4 * ib + j
                        c = W_M + 3 * j
                        for br in range(2):
                            pe.wait_ge(split, l * NW + W_M + 3 * i + br + 1 + SPLIT0)
                            for h in range(2):
                                pe.wait_ge(sig_done, l * 4 * KC + 4 * (i - 1) + 2 * br + h + 1 + SIG0)
                                t_half(c + br, range(KC), hT, 0, 2 * br, h).then_inc(g_done, 1)
                        pe.wait_ge(split, l * NW + W_M + 3 * i + 3 + SPLIT0)
                        pe.wait_ge(yg_l, (l + 1) * N_Z)
                        for br in range(2):
                            for h in range(2):
                                pe.wait_ge(mm_done, mm_no(l, i - 1, "AB"[br] + str(h)))
                                t_half(c + 2, range(4 * br, 4 * br + 4), (yg_hi, yg_lo), 4 * br,
                                       2 * br + 1, h).then_inc(yo_done, 1)
                for f in range(N_O):
                    if f % 2 == 0:
                        pe.wait_ge(split, l * NW + W_O + f + 2 + SPLIT0)
                    if f >= 4:
                        pe.wait_ge(x_new, l * KC + f - 3 + X_NEW0)
                    rows_unit(W_O + f - f % 2, (mg_hi, mg_lo), f % 2, f % 4,
                              (lambda k: pe.wait_ge(mg_l, l * 2 * KC + f * KC + k + 1)) if f < 2 else None
                              ).then_inc(o_done, 1)

        @block.scalar
        def _(act):
            copy = ACT.Copy
            for s, dst, src in ((rope_in, pos_i[:, :], positions.rearrange("b (m p) -> p (b m)", p=P)),
                                (rope_in, freq[:, :], rope_freq.rearrange("(a c) -> a c", a=1).to_broadcast([P, HALF])),
                                (table_in, table[:, :], rel_bias.rearrange("l h r -> (l h) r")),
                                (const_in, g_t, norm_g.rearrange("l (k p) -> p (l k)", p=P)),
                                (const_in, nsink, sinks.rearrange("l h -> (l h)").rearrange("(a c) -> a c", a=1)
                                 .to_broadcast([P, DEPTH * HEADS]))):
                with nc.allow_non_contiguous_dma(reason="a few KB"):
                    act.dma_start(dst, src).then_inc(s, 16)
            def exps(l, which, it, t):
                buf, cols, _ = scores(which, t)
                i = t % SB[which]
                end = cols.stop + (1 if which == "B" else 0)
                act.wait_ge(mx_done, tile_no(l, which, it, t) + 1)
                act.activation(buf[:, cols.start:end], buf[:, cols.start:end], ACT.Exp,
                               bias=nmax[:, i:i + 1], scale=-1.0,
                               accum_out=esum[:, i:i + 1]).then_inc(ex_done, 1)

            def p_hi(l, which, it, t):
                if is_first(it) and t == 0:
                    act.wait_ge(zero_set, 2 * l + 1 + ORDER[which])
                if t % 2 == 0 and not (is_first(it) and t // 2 < PT[which]):
                    act.wait_ge(av_done, pair_no(l, which, it, t // 2) - PT[which] + 1)
                for g, bank, first, k in groups(which, t):
                    act.wait_ge(tr_done, group_no(l, which, it, g) + 1)
                    act.activation(pt_hi[which][slots_of(which, t, first, k)],
                                   acc[:, bank, 0:k * P].rearrange("p (n c) -> p n c", c=P),
                                   copy).then_inc(ph_done, 1)

            def y_out(l, which, it, t):
                if t % 2 == 0:
                    return
                u, m = divmod(t, ST)
                a = m // 2
                if which == "A" and is_first(it) and t == 1:
                    for s in (NU - 2, NU - 1):
                        act.wait_ge(stored[s % 2], stored_after(l, s))
                act.wait_ge(av_done, pair_no(l, which, it, t // 2) + 1)
                if which == "A":
                    act.activation(y_rows(which, it, t), av_rows(which, t, 1 - u), copy).then_inc(y_half, 1)
                else:
                    act.activation(y_rows(which, it, t), av_rows(which, t, 0), copy).then_inc(y_done, 1)

            def stage(l, u, c, ib=0):
                act.wait_ge(st_lo, l * NU + u + 1)
                if UB - 2 <= c < UB:
                    act.wait_ge(vb_lo, l * 2 + c - UB + 3)
                half, s = c % 2, stored[c % 2]
                rows, tiles = slice(512 * half, 512 * half + 512), slice(4 * half, 4 * half + 4)
                for i, st in enumerate((stage_hi, stage_lo)):
                    src = st[:, c % 2, :].bitcast(F32)
                    by_row = src.rearrange("p (m h c) -> p m h c", m=4, c=HD)
                    if c < UB - 2:
                        for j in range(4):
                            act.dma_start(qB[4 * (c // 2) + j, i, :, rows],
                                          src[j % 2 * HD:j % 2 * HD + HD, j // 2 * 512:j // 2 * 512 + 512]
                                          ).then_inc(s, 16)
                    elif c < UB:
                        act.dma_start(kB[:, i, :, rows], src[:, 0:512]).then_inc(s, 16)
                        by_row = src[:, 512:1024].rearrange("p (m h c) -> p m h c", m=4, c=HD)
                        for j in range(KV_HEADS):
                            act.dma_start(vB[j, :, tiles, i, :], by_row[:, :, j, :]).then_inc(s, 16)
                    elif c < UB + UV:
                        for j in range(4):
                            act.dma_start(vA[4 * ((c - UB) // 2) + j, :, tiles, i, :], by_row[:, :, j, :]
                                          ).then_inc(s, 16)
                    else:
                        t = c - UB - UV
                        act.dma_start(qkA[ds(4 * ib + t // 2 * 2, 2), t % 2, i], src).then_inc(s, 16)

            def root(n, h):
                act.wait_ge(ms_done, 2 * n + h + 1)
                act.activation(rms[:, 4 * h:4 * h + 4], ssq[:, 4 * h:4 * h + 4], ACT.Sqrt).then_inc(rt_done, 1)

            def squares(m, c0, cols, part):
                act.activation(xs[:, m, c0:c0 + cols], xt[:, m, c0:c0 + cols], ACT.Square,
                               accum_out=part_sq[:, m, part:part + 1]).then_inc(sq_done, 1)

            def last_squares():
                for m in range(4, ST):
                    squares(m, 768, 256, 3)

            act.wait_ge(no_sq, 1)
            for m in range(ST):
                act.wait_ge(x_in[m], 16)
                squares(m, 0, D if m < 4 else 768, 0)
                if m == 3:
                    root(0, 0)
            act.wait_ge(tab, TAB_STEPS)
            act.activation(sin_t[:, :, :].rearrange("p m c -> p (m c)"), ang[:, 0, :], ACT.Sin).then_inc(tab_act, 1)
            act.activation(cos_t[:, :, :].rearrange("p m c -> p (m c)"), ang[:, 1, :], ACT.Sin).then_inc(tab_act, 1)
            act.wait_ge(ext_ready, 2)
            act.dma_start(ext_dram[:, 0:EXT], ext[:, :]).then_inc(ext_out, 16)

            with act.Fori(0, DEPTH) as l:
                act.wait_ge(g_set, l + 1)
                for i in range(2 * KC):
                    h, k = divmod(i, KC)
                    if i == KC:
                        act.wait_ge(x_new, l * KC + X_NEW0)
                        last_squares()
                        root(l, 1)
                    act.wait_ge(ht_ps, l * 2 * KC + i + 1)
                    act.activation(hT_hi[:, k, h * 512:h * 512 + 512], acc[:, 4 + k % 4 if h else k, :], copy,
                                   scale=g_now[:, k:k + 1]).then_inc(ht_hi, 1)
                act.wait_ge(ext_out, 16)
                for u in range(UB + UV):
                    if u >= 2:
                        act.wait_ge(stored[u % 2], stored_after(l, u - 2))
                    if u < UB - 2:
                        act.wait_ge(rt_ps, l * UB + u + 1)
                        act.activation(stage_hi[:, u % 2, :], flat(2 + u % 2), copy).then_inc(st_hi, 1)
                    elif u < UB:
                        act.wait_ge(rope_m, l * 2 * UB + 2 * u + 2)
                        act.activation(stage_hi[:, u % 2, 512:1024].rearrange("p (m c) -> p m c", m=4),
                                       flat(u % 2).rearrange("p (m c) -> p m c", m=4)[:, :, P:2 * P],
                                       copy).then_inc(vb_hi, 1)
                        act.wait_ge(rt_ps, l * UB + u + 1)
                        act.activation(stage_hi[:, u % 2, 0:512], pair(2 + u % 2)[:, 0, :], copy).then_inc(st_hi, 1)
                    else:
                        act.wait_ge(u_done, l * NU + u + 1)
                        act.activation(stage_hi[:, u % 2, :], flat(u % 2), copy).then_inc(st_hi, 1)
                    stage(l, u, u)
                act.activation(warm[:, 1:2], warm[:, 0:1], ACT.Exp)
                with act.Fori(0, N_T // 4) as ib:
                    for j in range(4):
                        c = UB + UV + j
                        act.wait_ge(stored[j % 2], stored_after(l, c - 2, 2 * ib))
                        act.wait_ge(u_done, l * NU + c + 4 * ib + 1)
                        act.activation(stage_hi[:, j % 2, :], flat(2 + j % 2), copy).then_inc(st_hi, 1)
                        stage(l, c + 4 * ib, c, ib)
                for which in "AB":
                    pipeline(act, "act", l, which, {"hi": p_hi, "exp": exps, "y": y_out})
                def gated_hi(b):
                    act.wait_ge(zy_done, l * N_Z + b + 1 + ZY0)
                    act.activation(yg_hi[:, ds(b, 1), :].rearrange("p a c -> p (a c)"),
                                   y_raw[:, ds(b, 1), :].rearrange("p a c -> p (a c)"), copy).then_inc(yg_h, 1)

                with act.Fori(0, N_Z // 4) as ib:
                    for j in range(4):
                        b = 4 * ib + j
                        act.wait_ge(z_done, l * N_Z + b + 1)
                        act.wait_ge(zy_done, l * N_Z + b + ZY0)
                        act.activation(sg[:, :], flat(j % 2), ACT.Silu).then_inc(silu_done, 1)
                        gated_hi(b)
                def sigmoid(i, br, h):
                    cols = slice(512 * h, 512 * h + 512)
                    act.wait_ge(g_done, l * 4 * KC + 4 * i + 2 * br + h + 1)
                    act.wait_ge(mm_done, mm_no(l, i, f"A{h}") if br else mm_no(l, i - 1, f"S{h}"))
                    act.activation(sg[:, cols], pair(2 * br)[:, h, :], ACT.Sigmoid).then_inc(sig_done, 1)

                def merged_hi(i, h):
                    cols = slice(512 * h, 512 * h + 512)
                    act.wait_ge(mm_done, mm_no(l, i, f"S{h}"))
                    act.activation(mg_hi[:, i, cols], merged[:, i, cols], copy).then_inc(mg_h, 1)

                with act.Fori(0, KC - 1) as i:
                    for br in range(2):
                        for h in range(2):
                            sigmoid(i, br, h)
                last = KC - 1
                sigmoid(last, 0, 0)
                sigmoid(last, 0, 1)
                act.wait_ge(g_done, (l + 1) * 4 * KC)
                for i in range(last):
                    if i == 4:
                        sigmoid(last, 1, 0)
                    merged_hi(i, 0)
                sigmoid(last, 1, 1)
                merged_hi(last, 0)
                for i in range(KC):
                    merged_hi(i, 1)
                for f in range(N_O - 1):
                    c, h = divmod(f, 2)
                    act.wait_ge(x_new, l * KC + f + 1 + X_NEW0)
                    for m in range(4 * h, 4 * h + 4):
                        squares(m, 256 * c, 256, c)
                root(l + 1, 0)
            act.wait_ge(x_new, DEPTH * KC + X_NEW0)
            last_squares()
            root(DEPTH, 1)

        @block.vector
        def _(dve):
            dve.wait_ge(rope_in, 32)
            n = [0]

            def step(ins):
                n[0] += 1
                ins.then_inc(tab, 1)
                dve.wait_ge(tab, n[0])

            a0, a1 = ang[:, 0, :], ang[:, 1, :]
            tn, tn_i, wr = turns[:, 0, :], turns_i[:, 0, :], wrap[:, 0, :]
            step(dve.tensor_copy(pos_f[:, :], pos_i[:, :]))
            step(dve.tensor_tensor(a0.rearrange("p (m c) -> p m c", m=ST),
                                   pos_f[:, :].unsqueeze(2).to_broadcast([P, ST, HALF]),
                                   freq[:, :].unsqueeze(1).to_broadcast([P, ST, HALF]), ALU.mult))
            step(dve.tensor_scalar(tn, a0, 1 / (2 * np.pi), None, ALU.mult))
            step(dve.tensor_copy(tn_i, tn))
            step(dve.tensor_copy(tn, tn_i))
            for part in PI2:
                step(dve.scalar_tensor_tensor(out=a0, in0=tn, scalar=-part, in1=a0, op0=ALU.mult, op1=ALU.add))
            for a, op, lim in ((a0, ALU.is_gt, np.pi), (a0, ALU.is_lt, -np.pi), (a1, ALU.is_gt, np.pi)):
                if a is a1:
                    step(dve.tensor_scalar(a1, a0, np.pi / 2, None, ALU.add))
                step(dve.tensor_scalar(wr, a, lim, -2 * lim, op, ALU.mult))
                step(dve.tensor_tensor(a, a, wr, ALU.add))
            step(dve.tensor_scalar(ang[:, :, :], ang[:, :, :], 3.1415925, -3.1415925, ALU.min, ALU.max))
            assert n[0] == TAB_STEPS
            dve.wait_ge(const_in, 32)
            step(dve.tensor_scalar(nsink, nsink, -1.0, None, ALU.mult))

            def buffer_free(l, which, it, t):
                if not (is_first(it) and t < SB[which]):
                    before = first_group(which, (t - SB[which]) % TILES + 1) - (GROUPS[which] if t < SB[which] else 0)
                    dve.wait_ge(tr_done, group_no(l, which, it, before))

            def sinks_of(l, which, it, t):
                if which == "B":
                    buf, cols, _ = scores(which, t)
                    buffer_free(l, which, it, t)
                    dve.sem_inc(held["dve"], 1)
                    dve.tensor_copy(buf[:, cols.stop:cols.stop + 1],
                                    nsink[:, ds(l * HEADS + 2 * it + t // ST, 1)]).then_inc(sk_done, 1)

            def maxes(l, which, it, t):
                buf, cols, nb = scores(which, t)
                no = tile_no(l, which, it, t)
                i = t % SB[which]
                b = bias[which][t // ST]
                if which == "A":
                    buffer_free(l, which, it, t)
                    start = 3e38
                else:
                    dve.wait_ge(sk_done, (l * HP + it) * TILES + t + 1)
                    start = buf[:, cols.stop:cols.stop + 1]
                hold("dve", dve, qk_done, no + 1)
                out_, in1, in0 = buf[:, cols], b[:, cols], qk_dst(which, t)[:, 0:nb * P]
                if nb * P > 512:
                    out_, in1 = [v.rearrange("p (h c) -> p h c", h=2) for v in (out_, in1)]
                    in0 = pair(t % 2)[:, :, 0:nb * P // 2]
                dve.tensor_tensor_reduce(out_, in0, in1, -SCALE, start, ALU.add, ALU.min,
                                         nmax[:, i:i + 1]).then_inc(mx_done, 1)

            def recips(l, which, it, t):
                i = t % SB[which]
                dve.wait_ge(ex_done, tile_no(l, which, it, t) + 1)
                dve.reciprocal(rinv[:, i:i + 1], esum[:, i:i + 1]).then_inc(ri_done, 1)

            def p_lo(l, which, it, t):
                for g, bank, first, k in groups(which, t):
                    where = slots_of(which, t, first, k)
                    dve.wait_ge(ph_done, group_no(l, which, it, g) + 1)
                    dve.tensor_tensor(pt_lo[which][where], acc[:, bank, 0:k * P].rearrange("p (n c) -> p n c", c=P),
                                      pt_hi[which][where].bitcast(F32), ALU.subtract).then_inc(pl_done, 1)

            def y_add(l, which, it, t):
                if t % 2 == 0:
                    return
                y = y_rows(which, it, t)
                dve.wait_ge(y_half, (l * HP + it) * PAIRS + t // 2 + 1)
                dve.tensor_tensor(y, av_rows(which, t, t // ST), y, ALU.add).then_inc(y_done, 1)

            def rope(l, u):
                h = u % 2
                wide = 8 if u < UB - 2 else 4
                ps = flat(h).rearrange("p (m g c) -> p m g c", m=4, c=HALF)[:, :, 0:wide, :]
                dve.wait_ge(u_done, l * NU + u + 1)
                for dst, tb in ((r_cos, cos_t), (r_sin, sin_t)):
                    dve.tensor_tensor(dst[:, :, :].rearrange("p m (g c) -> p m g c", c=HALF)[:, :, 0:wide, :], ps,
                                      tb[:, 4 * h:4 * h + 4, :].unsqueeze(2).to_broadcast([P, 4, wide, HALF]),
                                      ALU.mult).then_inc(rope_m, 1)
                dve.wait_ge(rope_m, l * 2 * UB + 2 * u + 2)
                if u >= 2:
                    dve.wait_ge(rt_ps, l * UB + u - 1)
                c4, s4, r4 = [v.rearrange("p m (g t c) -> p m g t c", t=2, c=HALF)[:, :, 0:wide // 2]
                              for v in (r_cos[:, :, :], r_sin[:, :, :], rot[:, u % 2])]
                dve.tensor_tensor(r4[:, :, :, 0], c4[:, :, :, 0], s4[:, :, :, 1], ALU.subtract).then_inc(rope_o, 1)
                dve.tensor_tensor(r4[:, :, :, 1], c4[:, :, :, 1], s4[:, :, :, 0], ALU.add).then_inc(rope_o, 1)
                dve.wait_ge(rope_o, l * 2 * UB + 2 * u + 2)

            def lo_of(l, u, c):
                s = c % 2
                dve.wait_ge(st_hi, l * NU + u + 1)
                hi, lo = stage_hi[:, s, :].bitcast(F32), stage_lo[:, s, :]
                if c < UB - 2:
                    dve.tensor_tensor(lo, flat(2 + s), hi, ALU.subtract).then_inc(st_lo, 1)
                elif c < UB:
                    dve.tensor_tensor(lo[:, 0:512], pair(2 + s)[:, 0, :], hi[:, 0:512],
                                      ALU.subtract).then_inc(st_lo, 1)
                else:
                    dve.tensor_tensor(lo, flat(s if c < UB + UV else 2 + s), hi, ALU.subtract).then_inc(st_lo, 1)

            def v_lo_of(l, u):
                s = u % 2
                dve.wait_ge(vb_hi, l * 2 + u - UB + 3)
                dve.tensor_tensor(stage_lo[:, s, 512:1024].rearrange("p (m c) -> p m c", m=4),
                                  flat(s).rearrange("p (m c) -> p m c", m=4)[:, :, P:2 * P],
                                  stage_hi[:, s, 512:1024].bitcast(F32).rearrange("p (m c) -> p m c", m=4),
                                  ALU.subtract).then_inc(vb_lo, 1)

            def inverse_root(n, h):
                squares = 4 if isinstance(n, int) and n == h == 0 else 8 + 32 * n + 4 * h
                four = slice(4 * h, 4 * h + 4)
                ms, y, t = ssq[:, four], rstd[:, four], rsq[:, four]
                dve.wait_ge(sq_done, squares)
                dve.tensor_reduce(ms, part_sq[:, four, :], mybir.AxisListType.X, ALU.add).then_inc(ms_in, 1)
                dve.wait_ge(ms_in, 2 * n + h + 1)
                dve.tensor_scalar(ms, ms, 1 / D, EPS, ALU.mult, ALU.add).then_inc(ms_done, 1)
                dve.wait_ge(rt_done, 2 * n + h + 1)
                for i, ins in enumerate((
                        lambda: dve.reciprocal(y, rms[:, four]),
                        lambda: dve.tensor_tensor(t, y, y, ALU.mult),
                        lambda: dve.tensor_tensor(t, t, ms, ALU.mult),
                        lambda: dve.tensor_scalar(t, t, -0.5, 1.5, ALU.mult, ALU.add),
                        lambda: dve.tensor_tensor(y, y, t, ALU.mult))):
                    ins().then_inc(rs_done, 1)
                    dve.wait_ge(rs_done, 5 * (2 * n + h) + i + 1)

            def over_rms(m):
                dve.tensor_scalar(xs[:, m, :], xt[:, m, :], rstd[:, m:m + 1], None, ALU.mult).then_inc(xs_done, 1)

            inverse_root(0, 0)
            for m in range(4):
                over_rms(m)
            dve.wait_ge(table_in, 16)
            far = SW - CHUNK * 2 + P - 1 - A_MAX_REL
            dve.tensor_scalar(ext[:, 0:far], table[:, TW - 1:TW].to_broadcast([DEPTH * HEADS, far]),
                              1 / SCALE, None, ALU.mult).then_inc(ext_ready, 1)
            dve.tensor_scalar(ext[:, far:EXT], table[:, TW - 1:TW - 1 - (EXT - far):-1], 1 / SCALE, None,
                              ALU.mult).then_inc(ext_ready, 1)
            dve.wait_ge(tab_act, 2)
            with dve.Fori(0, DEPTH) as l:
                dve.tensor_copy(g_now, g_t.rearrange("p (l k) -> p l k", l=DEPTH)[:, ds(l, 1), :]
                                .rearrange("p a k -> p (a k)")).then_inc(g_set, 1)
                for i in range(2 * KC):
                    h, k = divmod(i, KC)
                    cols = slice(h * 512, h * 512 + 512)
                    if i == KC:
                        inverse_root(l, 1)
                        for m in range(4, ST):
                            over_rms(m)
                    dve.wait_ge(ht_hi, l * 2 * KC + i + 1)
                    dve.scalar_tensor_tensor(out=hT_lo[:, k, cols], in0=acc[:, 4 + k % 4 if h else k, :],
                                             scalar=g_now[:, k:k + 1], in1=hT_hi[:, k, cols].bitcast(F32),
                                             op0=ALU.mult, op1=ALU.subtract).then_inc(ht_lo, 1)
                for u in range(UB):
                    rope(l, u)
                    if u >= 1:
                        lo_of(l, u - 1, u - 1)
                    if u >= UB - 2:
                        v_lo_of(l, u)
                for u in range(UB - 1, UB + UV):
                    lo_of(l, u, u)
                with dve.Fori(0, N_T // 4) as ib:
                    for j in range(4):
                        lo_of(l, UB + UV + 4 * ib + j, UB + UV + j)
                for which in "AB":
                    dve.wait_ge(mask_set, 2 * l + 1 + ORDER[which])
                    if which == "B":
                        dve.wait_ge(tr_done, group_no(l, "B", 0, 0))
                    pipeline(dve, "dve", l, which, {"sk": sinks_of, "lo": p_lo, "mx": maxes, "ri": recips, "ya": y_add})
                with dve.Fori(0, N_Z) as b:
                    y = y_raw[:, ds(b, 1), :].rearrange("p a c -> p (a c)")
                    dve.wait_ge(silu_done, l * N_Z + b + 1 + SILU0)
                    dve.wait_ge(y_done, pair_no(l + 1, "A", 0, 0))
                    dve.tensor_tensor(y, y, sg[:, :], ALU.mult).then_inc(zy_done, 1)
                    dve.wait_ge(yg_h, l * N_Z + b + 1)
                    dve.tensor_tensor(yg_lo[:, ds(b, 1), :].rearrange("p a c -> p (a c)"), y,
                                      yg_hi[:, ds(b, 1), :].rearrange("p a c -> p (a c)").bitcast(F32),
                                      ALU.subtract).then_inc(yg_l, 1)
                def product(i, br, h):
                    cols = slice(512 * h, 512 * h + 512)
                    mg = merged[:, ds(i, 1), cols].rearrange("p a c -> p (a c)")
                    dve.wait_ge(sig_done, l * 4 * KC + 4 * i + 2 * br + h + 1 + SIG0)
                    dve.wait_ge(yo_done, l * 4 * KC + 4 * i + 2 * br + h + 1)
                    dve.tensor_tensor(sg[:, cols] if br else mg, pair(2 * br + 1)[:, h, :], sg[:, cols],
                                      ALU.mult).then_inc(mm_done, 1)
                    if br:
                        dve.wait_ge(mm_done, mm_no(l, i, f"B{h}"))
                        dve.tensor_tensor(mg, mg, sg[:, cols], ALU.add).then_inc(mm_done, 1)

                def merged_lo(i, h):
                    cols = slice(512 * h, 512 * h + 512)
                    dve.wait_ge(mg_h, l * 2 * KC + h * KC + i + 1)
                    dve.tensor_tensor(mg_lo[:, i, cols], merged[:, i, cols], mg_hi[:, i, cols].bitcast(F32),
                                      ALU.subtract).then_inc(mg_l, 1)

                with dve.Fori(0, KC - 1) as i:
                    for br in range(2):
                        for h in range(2):
                            product(i, br, h)
                last = KC - 1
                product(last, 0, 0)
                product(last, 0, 1)
                for i in range(last):
                    merged_lo(i, 0)
                product(last, 1, 0)
                merged_lo(last, 0)
                product(last, 1, 1)
                for i in range(KC):
                    merged_lo(i, 1)
                dve.wait_ge(x_back, 16 * ST * (l + 1))
                for f in range(N_O):
                    c0, h = 256 * (f // 2), f % 2
                    dve.wait_ge(o_done, l * KC + f + 1 + O_DONE0)
                    xv = xt[:, 4 * h:4 * h + 4, c0:c0 + 256]
                    dve.tensor_tensor(xv, flat(f % 4).rearrange("p (m c) -> p m c", m=4), xv,
                                      ALU.add).then_inc(x_new, 1)
                    if f == N_O - 2:
                        inverse_root(l + 1, 0)
                        for m in range(4):
                            over_rms(m)
            dve.wait_ge(gain_in, 16)
            for m in range(ST):
                if m == 4:
                    inverse_root(DEPTH, 1)
                if m < 4:
                    dve.wait_ge(xs_done, DEPTH * ST + m + 1)
                    dve.tensor_tensor(xs[:, m, :], xs[:, m, :], g_row[:, :], ALU.mult).then_inc(fin_y, 1)
                else:
                    dve.scalar_tensor_tensor(out=xs[:, m, :], in0=xt[:, m, :], scalar=rstd[:, m:m + 1],
                                             in1=g_row[:, :], op0=ALU.mult, op1=ALU.mult).then_inc(fin_y, 1)


_INS = ["x", "positions", "norm_g", "w_in", "rel_bias", "sinks", "w_a_out", "w_b_out", "w_out", "final_g"]


def kernel(**inputs):
    import concourse.bacc as _bacc
    from concourse.bass_utils import run_bass_kernel_spmd as _run

    nc = _bacc.Bacc("TRN2", target_bir_lowering=False, num_devices=1)
    arrays, args = {}, []
    values = [(name, np.ascontiguousarray(inputs[name])) for name in _INS]
    values.append(("rope_freq", (ROPE_THETA ** (-np.arange(HALF) / HALF)).astype(np.float32)))
    for name, a in values:
        arrays[f"in_{name}"] = a
        args.append(nc.dram_tensor(f"in_{name}", a.shape, mybir.dt.from_np(a.dtype), kind="ExternalInput").ap())
    out = nc.dram_tensor("out_0", (1, SEQ, D), F32, kind="ExternalOutput").ap()
    build(nc, *args, out)
    r = _run(nc, [arrays], core_ids=[0])
    return r.results[0]["out_0"]
```
